# Optimizing a Trainium2 kernel written in Bass

```python
import math, functools
import jax, jax.numpy as jnp
from jax import lax
import numpy as np

D_MODEL = 1024
BATCH = 1
SEQ = 1024
DEPTH = 1
DEC_BATCH = 8
DEC_SEQ = 1
PAST_LEN = 512
PAGE_SIZE = 128

N_META = 16
N_HEADS = 16
N_KV_HEADS = 4
HEAD_DIM = 64
ATTN_WIDTH = N_HEADS * HEAD_DIM
IDX_HEADS = 4
IDX_DIM = 64
TOP_K_MAX = 256
Q_BLOCK = 128
D_INNER = 2 * D_MODEL
SSD_HEAD_DIM = 64
SSD_HEADS = D_INNER // SSD_HEAD_DIM
SSD_GROUPS = 4
HEADS_PER_GROUP = SSD_HEADS // SSD_GROUPS
D_STATE = 128
CONV_W = 4
CONV_DIM = D_INNER + 2 * SSD_GROUPS * D_STATE
CHUNK = 128
D_FF = ((8 * D_MODEL // 3 + 127) // 128) * 128
EPS = 1e-6
IN_SPLITS = (ATTN_WIDTH, N_KV_HEADS * HEAD_DIM, N_KV_HEADS * HEAD_DIM, IDX_HEADS * IDX_DIM, IDX_DIM, IDX_HEADS,
             D_INNER, CONV_DIM, SSD_HEADS, D_MODEL, D_MODEL)
IN_COLS = sum(IN_SPLITS)

kernel_name = "hybrid_dsa_ssd_macaron_step"

def rmsnorm(x, g):
    xf = x.astype(jnp.float32)
    y = xf * lax.rsqrt(jnp.mean(xf * xf, axis=-1, keepdims=True) + EPS)
    return (y * g.astype(jnp.float32)).astype(x.dtype)

def swiglu(x, g, w_gate, w_up, w_down):
    h = rmsnorm(x, g)
    return (jax.nn.silu(h @ w_gate) * (h @ w_up)) @ w_down

def index_scores(qi, ki, wi, qpos, kpos):
    dots = jnp.einsum('bqhd,bsd->bqhs', qi, ki).astype(jnp.float32) * IDX_DIM ** -0.5
    score = jnp.einsum('bqh,bqhs->bqs', wi.astype(jnp.float32) * IDX_HEADS ** -0.5, jax.nn.relu(dots))
    return jnp.where(kpos[None, None, :] <= qpos[None, :, None], score, -jnp.inf)

def sparse_attend(q, ks, vs, valid):
    b, nq = q.shape[:2]
    qg = q.reshape(b, nq, N_KV_HEADS, N_HEADS // N_KV_HEADS, HEAD_DIM)
    s = jnp.einsum('bqhgd,bqnhd->bqhgn', qg, ks).astype(jnp.float32) * HEAD_DIM ** -0.5
    s = jnp.where(valid[:, :, None, None, :], s, -jnp.inf)
    p = jax.nn.softmax(s, axis=-1).astype(vs.dtype)
    o = jnp.einsum('bqhgn,bqnhd->bqhgd', p, vs)
    return o.reshape(b, nq, ATTN_WIDTH)

def dsa_prompt(q, k, v, qi, ki, wi):
    b, L = q.shape[:2]
    k_top = min(TOP_K_MAX, L // 4)
    n_blk = -(-L // Q_BLOCK)
    pad = n_blk * Q_BLOCK - L

    def blocks(a):
        a = jnp.pad(a, [(0, 0), (0, pad)] + [(0, 0)] * (a.ndim - 2))
        return jnp.moveaxis(a.reshape((b, n_blk, Q_BLOCK) + a.shape[2:]), 1, 0)

    kpos = jnp.arange(L)
    bidx = jnp.arange(b)[:, None, None]

    def one_block(args):
        qb, qib, wib, start = args
        qpos = start + jnp.arange(Q_BLOCK)
        _, idx = lax.top_k(index_scores(qib, ki, wib, qpos, kpos), k_top)
        valid = idx <= qpos[None, :, None]
        return sparse_attend(qb, k[bidx, idx], v[bidx, idx], valid)

    starts = jnp.arange(n_blk) * Q_BLOCK
    out = lax.map(one_block, (blocks(q), blocks(qi), blocks(wi), starts))
    return jnp.moveaxis(out, 0, 1).reshape(b, n_blk * Q_BLOCK, ATTN_WIDTH)[:, :L]

def dsa_sample(q, k, v, qi, ki, wi, cache_k, cache_v, cache_ki, page_table):
    b, T = q.shape[:2]
    P = page_table.shape[1] * PAGE_SIZE
    S = P + T
    k_top = min(TOP_K_MAX, S // 4)
    ki_all = jnp.concatenate([cache_ki[page_table].reshape(b, P, IDX_DIM), ki.astype(cache_ki.dtype)], axis=1)
    qpos = P + jnp.arange(T)
    _, idx = lax.top_k(index_scores(qi, ki_all, wi, qpos, jnp.arange(S)), k_top)
    valid = idx <= qpos[None, :, None]
    bidx = jnp.arange(b)[:, None, None]
    pidx = jnp.minimum(idx, P - 1)
    phys = page_table[bidx, pidx // PAGE_SIZE]
    off = pidx % PAGE_SIZE
    nidx = jnp.clip(idx - P, 0, T - 1)
    from_past = (idx < P)[..., None, None]
    ks = jnp.where(from_past, cache_k[phys, off], k[bidx, nidx])
    vs = jnp.where(from_past, cache_v[phys, off], v[bidx, nidx])
    return sparse_attend(q, ks, vs, valid)

def causal_conv(xbc, prev, w, bias):
    T = xbc.shape[1]
    xp = jnp.concatenate([prev.astype(xbc.dtype), xbc], axis=1)
    out = bias
    for j in range(CONV_W):
        out = out + xp[:, j:j + T] * w[j]
    return jax.nn.silu(out), xp[:, xp.shape[1] - (CONV_W - 1):]

def ssd_scan(x, dt, A, Bm, Cm, h0, chunk):
    b, T, G, E, P = x.shape
    N = Bm.shape[-1]
    nc = T // chunk
    f32 = jnp.float32
    x = x.astype(f32).reshape(b, nc, chunk, G, E, P)
    dt = dt.reshape(b, nc, chunk, G, E)
    Bm = Bm.astype(f32).reshape(b, nc, chunk, G, N)
    Cm = Cm.astype(f32).reshape(b, nc, chunk, G, N)
    acs = jnp.cumsum(dt * A, axis=2)
    causal = jnp.tril(jnp.ones((chunk, chunk), bool))
    seg = acs[:, :, :, None] - acs[:, :, None, :]
    Lmat = jnp.exp(jnp.where(causal[:, :, None, None], seg, -jnp.inf))
    CB = jnp.einsum('bzign,bzjgn->bzijg', Cm, Bm)
    M = CB[..., None] * Lmat * dt[:, :, None]
    y_diag = jnp.einsum('bzijge,bzjgep->bzigep', M, x)
    xw = x * (jnp.exp(acs[:, :, -1:] - acs) * dt)[..., None]
    states = jnp.einsum('bzjgn,bzjgep->bzgepn', Bm, xw)
    chunk_decay = jnp.exp(acs[:, :, -1])

    def step(h, inp):
        s, d = inp
        return h * d[..., None, None] + s, h

    h_last, h_prev = lax.scan(step, h0.astype(f32), (jnp.moveaxis(states, 1, 0), jnp.moveaxis(chunk_decay, 1, 0)))
    h_prev = jnp.moveaxis(h_prev, 0, 1)
    y_off = jnp.einsum('bzign,bzgepn->bzigep', Cm, h_prev) * jnp.exp(acs)[..., None]
    return (y_diag + y_off).reshape(b, T, G, E, P), h_last

def ssd_mixer(xbc, dt_raw, z, h0, dt_bias, a_log, d_skip, g_norm, pad_front, chunk):
    b, T = xbc.shape[:2]
    f32 = jnp.float32
    xs, Bm, Cm = jnp.split(xbc, [D_INNER, D_INNER + SSD_GROUPS * D_STATE], axis=-1)
    xs = xs.astype(f32).reshape(b, T, SSD_GROUPS, HEADS_PER_GROUP, SSD_HEAD_DIM)
    Bm = Bm.reshape(b, T, SSD_GROUPS, D_STATE)
    Cm = Cm.reshape(b, T, SSD_GROUPS, D_STATE)
    dt = jax.nn.softplus(dt_raw.astype(f32) + dt_bias.astype(f32)).reshape(b, T, SSD_GROUPS, HEADS_PER_GROUP)
    A = -jnp.exp(a_log.astype(f32)).reshape(SSD_GROUPS, HEADS_PER_GROUP)
    pad_back = (-(pad_front + T)) % chunk

    def padt(a):
        return jnp.pad(a, [(0, 0), (pad_front, pad_back)] + [(0, 0)] * (a.ndim - 2))

    h0g = h0.reshape(b, SSD_GROUPS, HEADS_PER_GROUP, SSD_HEAD_DIM, D_STATE)
    y, h_last = ssd_scan(padt(xs), padt(dt), A, padt(Bm), padt(Cm), h0g, chunk)
    y = y[:, pad_front:pad_front + T] + d_skip.astype(f32).reshape(SSD_GROUPS, HEADS_PER_GROUP)[:, :, None] * xs
    y = y.reshape(b, T, D_INNER) * jax.nn.silu(z.astype(f32))
    yg = y.reshape(b, T, SSD_GROUPS, D_INNER // SSD_GROUPS)
    yg = yg * lax.rsqrt(jnp.mean(yg * yg, axis=-1, keepdims=True) + EPS)
    y = yg.reshape(b, T, D_INNER) * g_norm.astype(f32)
    return y.astype(xbc.dtype), h_last.reshape(b, SSD_HEADS, SSD_HEAD_DIM, D_STATE).astype(h0.dtype)

def layer_forward(x, attend, conv_prev, h0, pad_front, chunk,
                  g_ffn1, w_ffn1_gate, w_ffn1_up, w_ffn1_down, g_mix, w_in, g_q, g_k,
                  conv_w, conv_b, dt_bias, a_log, d_skip, g_ssd_norm,
                  w_attn_out, w_ssd_out, w_o, g_ffn2, w_ffn2_gate, w_ffn2_up, w_ffn2_down):
    x = x + 0.5 * swiglu(x, g_ffn1, w_ffn1_gate, w_ffn1_up, w_ffn1_down)
    h = rmsnorm(x, g_mix)
    b, T = h.shape[:2]
    offsets = np.cumsum(IN_SPLITS)[:-1].tolist()
    q, k, v, qi, ki, wi, z, xbc, dt_raw, ga, gs = jnp.split(h @ w_in, offsets, axis=-1)
    q = rmsnorm(q.reshape(b, T, N_HEADS, HEAD_DIM), g_q)
    k = rmsnorm(k.reshape(b, T, N_KV_HEADS, HEAD_DIM), g_k)
    v = v.reshape(b, T, N_KV_HEADS, HEAD_DIM)
    qi = qi.reshape(b, T, IDX_HEADS, IDX_DIM)
    attn = attend(q, k, v, qi, ki, wi)
    xbc, conv_state = causal_conv(xbc, conv_prev, conv_w, conv_b)
    ssd, ssm_state = ssd_mixer(xbc, dt_raw, z, h0, dt_bias, a_log, d_skip, g_ssd_norm, pad_front, chunk)
    mixed = jax.nn.sigmoid(ga) * (attn @ w_attn_out) + jax.nn.sigmoid(gs) * (ssd @ w_ssd_out)
    x = x + mixed @ w_o
    x = x + 0.5 * swiglu(x, g_ffn2, w_ffn2_gate, w_ffn2_up, w_ffn2_down)
    return x, k, v, ki, ssm_state, conv_state

def setup_inputs(seed: int = 0) -> dict:
    key = jax.random.key(seed)
    keys = iter(jax.random.split(key, 40))

    def nrm(shape, scale=1.0):
        return scale * jax.random.normal(next(keys), shape, jnp.float32)

    def gain(shape):
        return 1.0 + nrm(shape, 0.05)

    n_pages = PAST_LEN // PAGE_SIZE
    n_used = DEC_BATCH * n_pages
    n_pool = n_used + (n_used + 3) // 4
    page_table = jax.random.permutation(next(keys), n_pool)[:n_used].reshape(DEC_BATCH, n_pages).astype(jnp.int32)
    dt0 = jnp.exp(jax.random.uniform(next(keys), (DEPTH, SSD_HEADS), jnp.float32, math.log(1e-3), math.log(1e-1)))
    dt_bias = dt0 + jnp.log(-jnp.expm1(-dt0))
    a_log = jnp.log(jax.random.uniform(next(keys), (DEPTH, SSD_HEADS), jnp.float32, 1.0, 16.0))
    return {
        "x_prompt": nrm((BATCH, SEQ, D_MODEL)),
        "x_sample": nrm((DEC_BATCH, DEC_SEQ, D_MODEL)),
        "cache_k": nrm((DEPTH, n_pool, PAGE_SIZE, N_KV_HEADS, HEAD_DIM)),
        "cache_v": nrm((DEPTH, n_pool, PAGE_SIZE, N_KV_HEADS, HEAD_DIM)),
        "cache_kidx": nrm((DEPTH, n_pool, PAGE_SIZE, IDX_DIM)),
        "state_ssm": nrm((DEPTH, DEC_BATCH, SSD_HEADS, SSD_HEAD_DIM, D_STATE), 0.1),
        "state_conv": nrm((DEPTH, DEC_BATCH, CONV_W - 1, CONV_DIM)),
        "page_table": page_table,
        "meta_tokens": nrm((N_META, D_MODEL)),
        "g_ffn1": gain((DEPTH, D_MODEL)),
        "w_ffn1_gate": nrm((DEPTH, D_MODEL, D_FF), D_MODEL ** -0.5),
        "w_ffn1_up": nrm((DEPTH, D_MODEL, D_FF), D_MODEL ** -0.5),
        "w_ffn1_down": nrm((DEPTH, D_FF, D_MODEL), D_FF ** -0.5),
        "g_mix": gain((DEPTH, D_MODEL)),
        "w_in": nrm((DEPTH, D_MODEL, IN_COLS), D_MODEL ** -0.5),
        "g_q": gain((DEPTH, HEAD_DIM)),
        "g_k": gain((DEPTH, HEAD_DIM)),
        "conv_w": nrm((DEPTH, CONV_W, CONV_DIM), CONV_W ** -0.5),
        "conv_b": nrm((DEPTH, CONV_DIM), 0.02),
        "dt_bias": dt_bias,
        "a_log": a_log,
        "d_skip": gain((DEPTH, SSD_HEADS)),
        "g_ssd_norm": gain((DEPTH, D_INNER)),
        "w_attn_out": nrm((DEPTH, ATTN_WIDTH, D_MODEL), ATTN_WIDTH ** -0.5),
        "w_ssd_out": nrm((DEPTH, D_INNER, D_MODEL), D_INNER ** -0.5),
        "w_o": nrm((DEPTH, D_MODEL, D_MODEL), D_MODEL ** -0.5),
        "g_ffn2": gain((DEPTH, D_MODEL)),
        "w_ffn2_gate": nrm((DEPTH, D_MODEL, D_FF), D_MODEL ** -0.5),
        "w_ffn2_up": nrm((DEPTH, D_MODEL, D_FF), D_MODEL ** -0.5),
        "w_ffn2_down": nrm((DEPTH, D_FF, D_MODEL), D_FF ** -0.5),
    }

def reference(x_prompt, x_sample, cache_k, cache_v, cache_kidx, state_ssm, state_conv, page_table,
              meta_tokens, g_ffn1, w_ffn1_gate, w_ffn1_up, w_ffn1_down, g_mix, w_in, g_q, g_k,
              conv_w, conv_b, dt_bias, a_log, d_skip, g_ssd_norm, w_attn_out, w_ssd_out, w_o,
              g_ffn2, w_ffn2_gate, w_ffn2_up, w_ffn2_down):
    b = x_prompt.shape[0]
    xp = jnp.concatenate([jnp.broadcast_to(meta_tokens[None].astype(x_prompt.dtype), (b, N_META, D_MODEL)), x_prompt], axis=1)
    xs = x_sample
    kp, vp, kip, hp, cp = [], [], [], [], []
    ks, vs, kis, hs, cs = [], [], [], [], []
    for l in range(DEPTH):
        lw = (g_ffn1[l], w_ffn1_gate[l], w_ffn1_up[l], w_ffn1_down[l], g_mix[l], w_in[l], g_q[l], g_k[l],
              conv_w[l], conv_b[l], dt_bias[l], a_log[l], d_skip[l], g_ssd_norm[l],
              w_attn_out[l], w_ssd_out[l], w_o[l], g_ffn2[l], w_ffn2_gate[l], w_ffn2_up[l], w_ffn2_down[l])
        xp, k1, v1, ki1, h1, c1 = layer_forward(
            xp, dsa_prompt, jnp.zeros((b, CONV_W - 1, CONV_DIM), xp.dtype),
            jnp.zeros((b, SSD_HEADS, SSD_HEAD_DIM, D_STATE), xp.dtype), (-N_META) % CHUNK, CHUNK, *lw)
        kp.append(k1); vp.append(v1); kip.append(ki1); hp.append(h1); cp.append(c1)
        attend_s = functools.partial(dsa_sample, cache_k=cache_k[l], cache_v=cache_v[l],
                                     cache_ki=cache_kidx[l], page_table=page_table)
        xs, k2, v2, ki2, h2, c2 = layer_forward(
            xs, attend_s, state_conv[l], state_ssm[l], 0, min(CHUNK, xs.shape[1]), *lw)
        ks.append(k2); vs.append(v2); kis.append(ki2); hs.append(h2); cs.append(c2)
    y_prompt = xp[:, N_META:]
    y_sample = xs
    return (y_prompt, y_sample,
            jnp.stack(kp), jnp.stack(vp), jnp.stack(kip), jnp.stack(hp), jnp.stack(cp),
            jnp.stack(ks), jnp.stack(vs), jnp.stack(kis), jnp.stack(hs), jnp.stack(cs))


_drawn_inputs = setup_inputs


def setup_inputs(seed=0):
    import zlib

    import numpy as np

    out = dict(_drawn_inputs(seed))
    spreads = {}
    factors = {'g_q': 8.0, 'd_skip': 5.453, 'g_ffn2': 3.16}
    for name, (base, spread) in spreads.items():
        noise = np.random.default_rng([zlib.crc32(name.encode()), seed]).standard_normal(out[name].shape)
        drawn = base * np.exp(spread * noise) if base else spread * noise
        out[name] = __import__('jax').numpy.asarray(drawn.astype(out[name].dtype))
    for name, factor in factors.items():
        out[name] = (out[name] * factor).astype(out[name].dtype)
    return out
```

```python
from contextlib import ExitStack

import concourse.bass as bass
from concourse import mybir

ALU = mybir.AluOpType
ACT = mybir.ActivationFunctionType
F32 = mybir.dt.float32
F32R = mybir.dt.float32r
BF16 = mybir.dt.bfloat16
I32 = mybir.dt.int32
U32 = mybir.dt.uint32
AX_X = mybir.AxisListType.X

P = 128
D = 1024
KD = D // P
META, SEQ, NS = 16, 1024, 8
L = META + SEQ
T = L + NS
NT = (L + P - 1) // P
LAST = L - (NT - 1) * P
CH = [(0, 352), (352, 352), (704, T - 704)]
HD, NH, NKV = 64, 16, 4
TOPK = min(256, L // 4)
PAGES, PS = 4, 128
PAST = PAGES * PS
TOPK_S = min(256, (PAST + 1) // 4)
DI, DSTATE, SH, SG = 2048, 128, 32, 4
CONVD = DI + 2 * SG * DSTATE
DFF = 2816
NF = DFF // P
EPS = 1e-6
MASKED = -1e30
TAKEN = -3e38
COL = dict(q=0, k=1024, v=1280, qi=1536, kiwi=1792, z=1860, xbc=3908, dt=6980, ga=7012, gs=8036)

FFN_TILES = 3 * NF
N_IN = 16 + 16 + 8 + 8 + 24
TILE_FFN1 = 0
TILE_IN = FFN_TILES
TILE_AO = TILE_IN + N_IN
TILE_SO = TILE_AO + 8
TILE_WO = TILE_SO + 16
TILE_FFN2 = TILE_WO + 8
ORD_FFN1 = 0
ORD_IN = NF
ORD_AO = ORD_IN + N_IN // 2
ORD_SO = ORD_AO + 4
ORD_WO = ORD_SO + 8
ORD_FFN2 = ORD_WO + 4


class Chain:

    def __init__(self, eng, sem):
        self.eng, self.sem, self.n = eng, sem, 0

    def step(self, ins):
        ins.then_inc(self.sem, 1)
        self.n = self.n + 1
        return ins

    def run(self, ins):
        self.step(ins)
        self.settle()

    def settle(self):
        self.eng.wait_ge(self.sem, self.n)


def build(nc, A, O):
    ctx = ExitStack()
    with ctx:
        ctx.enter_context(nc.allow_non_contiguous_dma(reason="small parameter vectors"))

        def sem(name):
            return ctx.enter_context(nc.semaphore(name))

        BASE = 16512
        top = {}

        def at(name, shape, dt=F32, off=0):
            return nc.alloc_sbuf_tensor_at(name, shape, dt, offset=off)

        class Region:
            def __init__(self, off, size):
                self.off, self.end, self.cur = off, off + size, off

            def take(self, name, shape, dt=F32):
                n = 1
                for s in shape[1:]:
                    n *= s
                n = (n * (2 if dt == BF16 else 4) + 31) // 32 * 32
                t = at(name, shape, dt, self.cur)
                self.cur += n
                assert self.cur <= self.end, (name, self.cur - self.end)
                return t

        XB = KD * T * 4
        r = Region(BASE, 229344 - BASE)
        hhi = r.take("hhi", [P, KD, T], F32R)
        hlo = r.take("hlo", [P, KD, T], F32R)
        R1 = r.cur
        X = r.take("X", [P, KD, T])
        wraw = r.take("wraw", [P, 2, 1024])
        WHI = r.cur
        whi = r.take("whi", [P, 2, 1024], F32R)
        wlo = r.take("wlo", [P, 2, 1024], F32R)
        ident = r.take("ident", [P, P])
        ones = r.take("ones", [P, P])
        blk = r.take("blk", [P, P])
        tri = r.take("tri", [P, P])
        delta8 = r.take("delta8", [P, NS, NS])
        hm = r.take("hm", [P, 2])
        rep = r.take("rep", [NS, P])
        g1 = r.take("g1", [P, KD])
        gm = r.take("gm", [P, KD])
        g2 = r.take("g2", [P, KD])
        gq = r.take("gq", [P, 1])
        gk = r.take("gk", [P, 1])
        cw = r.take("cw", [P, CONVD // P, 4])
        cb = r.take("cb", [P, CONVD // P])
        gssd = r.take("gssd", [P, DI // P])
        dsk = r.take("dsk", [P, DI // P])
        eps = r.take("eps", [P, 1])
        dtb = r.take("dtb", [SH, 1])
        nega = r.take("nega", [SH, 1])
        ptab = r.take("ptab", [P, NS * PAGES], I32)
        pidx = r.take("pidx", [P, NS * PAGES], U32)
        piota = r.take("piota", [P, 1], I32)
        piotaf = r.take("piotaf", [P, 1])
        wi9 = r.take("wi9", [P, NT, 4])
        qis = r.take("qis", [P, 2, NS])
        kxs = r.take("kxs", [P, NS])
        kis = r.take("kis", [NS, 68])
        ksam = r.take("ksam", [NS, 256])
        vsam = r.take("vsam", [NS, 256])
        AR = r.cur
        AEND = r.end
        a = Region(AR, AEND - AR)
        sq = a.take("sq", [P, KD, 352])
        hf = a.take("hf", [P, KD, 352])
        rt = a.take("rt", [P, 3, 352])
        rs = a.take("rs", [P, 3, 352])
        whid = at("whid", [P, 2, 1024], F32R, AR)
        wlod = at("wlod", [P, 2, 1024], F32R, AR + 8192)
        XIN = a.cur
        hidhi = a.take("hidhi", [P, 2, T], F32R)
        hidlo = a.take("hidlo", [P, 2, T], F32R)
        sg = a.take("sg", [P, T])
        hidf = a.take("hidf", [P, T])
        xin = Region(XIN, AEND - XIN).take("xin", [P, NT, D])
        qT = at("qT", [P, KD, T], F32, R1)
        a = Region(AR, AEND - AR)
        kT = a.take("kT", [P, 2, T])
        vtok = a.take("vtok", [P, NT, 256])
        dtT = a.take("dtT", [SH, T])
        WID = [min(P * (t + 1), L) for t in range(NT)]
        MOFF = [sum(WID[:t]) for t in range(NT)]
        mboff = a.cur
        mb = a.take("mb", [P, sum(WID)], BF16)
        kit = at("kit", [P, NT, 68], F32, mboff)
        TREG = a.cur
        qiT = a.take("qiT", [P, 2, T])
        kiwi = a.take("kiwi", [P, T])
        ki2 = a.take("ki2", [P, T])
        vT_off = a.cur
        relu = a.take("relu", [P, 2, T])
        vT = at("vT", [P, 2, T], F32, vT_off)
        a2 = Region(TREG, AEND - TREG)
        XR = 1052
        spill = a2.take("spill", [P, 2, T])
        xraw = a2.take("xraw", [P, 2, XR])
        cv = a2.take("cv", [P, 2, T])
        SCR = max(a2.cur, a.cur)
        a = Region(SCR, AEND - SCR)
        SOFF = {t: sum(WID[2:t]) for t in range(2, NT)}
        sc = a.take("sc", [P, sum(WID[2:])])
        a = Region(SCR, AEND - SCR)
        nsq = a.take("nsq", [P, 2, 352])
        nrt = a.take("nrt", [P, 2, 352])
        nrs = a.take("nrs", [P, 352])
        a = Region(SCR, AEND - SCR)
        rtail = a.take("rtail", [P, CONVD // P, 24])
        top8 = at("top8", [P, 8], F32, AEND - 64)
        held = at("held", [P, 1], F32, AEND - 96)
        held2 = at("held2", [P, 1], F32, AEND - 128)
        a = Region(TREG, AEND - TREG)
        SMP = a.cur
        smx = a.take("smx", [P, 2, L])
        pr = a.take("pr", [P, 2, L])
        ptT = a.take("ptT", [P, 2, NT, P])
        otok = a.take("otok", [P, 2, D])
        kout_off = a.cur
        kout = a.take("kout", [P, NT, 256])
        nmax = a.take("nmax", [P, 2])
        lsum = a.take("lsum", [P, 2])
        rl = a.take("rl", [P, 2])
        kidxg = at("kidxg", [P, NS * PAGES, HD], F32, kout_off)
        vflat = at("vflat", [1, NS, 256], F32, kout_off)
        kg = at("kg", [P, NS * PAGES, 256], F32, BASE)
        vg = at("vg", [P, NS * PAGES, 256], F32, BASE + NS * PAGES * 1024)
        a = Region(SMP, kout_off - SMP)
        kxT = a.take("kxT", [P, 2, PAST])
        kgT = a.take("kgT", [P, 2, 2, PAST])
        qz = a.take("qz", [P, 2, NS, NS])
        qzz = a.take("qzz", [P, 2 * NS, P])
        SW = PAST + 8
        scs = a.take("scs", [NS, SW])
        relus = a.take("relus", [NS, SW])
        mss = a.take("mss", [NS, SW])
        ss_ = a.take("ss_", [P, SW])
        ps_ = a.take("ps_", [P, SW])
        ptS = a.take("ptS", [P, PAGES, P])
        pnT = a.take("pnT", [1, P])
        dg = a.take("dg", [NS, NS])
        smn = a.take("smn", [P, 4])
        xD = nc.dram_tensor("xD", (D, T), F32).ap()
        zD = nc.dram_tensor("zD", (DI, T), F32).ap()
        gaD = nc.dram_tensor("gaD", (D, T), F32).ap()
        gsD = nc.dram_tensor("gsD", (D, T), F32).ap()
        xcD = nc.dram_tensor("xcD", (CONVD, T), F32).ap()
        acsD = nc.dram_tensor("acsD", (SH, T), F32).ap()
        sD = nc.dram_tensor("sD", (DI, T), F32).ap()
        smD = nc.dram_tensor("smD", (2, SH, NS), F32).ap()
        bcD = nc.dram_tensor("bcD", (NS, 2 * SG * DSTATE), F32).ap()
        vnD = O["v_sample"]

        setA = ctx.enter_context(nc.psum_tensor("setA", [P, 3, 512], F32))
        setB = ctx.enter_context(nc.psum_tensor("setB", [P, 3, 512], F32))
        bankC = ctx.enter_context(nc.psum_tensor("bankC", [P, 512], F32))
        bankD = ctx.enter_context(nc.psum_tensor("bankD", [P, 512], F32))
        SETS = [setA, setB]
        CD = [bankC, bankD]

        const_ready = sem("const_ready")
        pool_seq = sem("pool_seq")
        dve_seq = sem("dve_seq")
        params_loaded = sem("params_loaded")
        x_loaded = [sem(f"x_loaded{i}") for i in range(3)]
        xT_done = sem("xT_done")
        xT_evac = sem("xT_evac")
        raw_loaded = [sem("raw_loaded0"), sem("raw_loaded1")]
        w_hi = sem("w_hi")
        w_split = sem("w_split")
        gemm_done = [sem("gemm_doneA"), sem("gemm_doneB")]
        gemm_evac = [sem("gemm_evacA"), sem("gemm_evacB")]
        sq_done = sem("sq_done")
        ss_done = sem("ss_done")
        rt_done = sem("rt_done")
        h_ready = sem("h_ready")
        hid_mult = sem("hid_mult")
        hid_ready = sem("hid_ready")
        down_done = sem("down_done")
        down_evac = sem("down_evac")
        x_spilled = sem("x_spilled")
        outs_done = sem("outs_done")
        N_OUT = [0]

        def store(eng, dst, src):
            N_OUT[0] += 1
            return eng.dma_start(dst, src).then_inc(outs_done, 16)

        def trow(t):
            return t * P, (P if t < NT - 1 else LAST), (P if t < NT - 1 else LAST + NS)

        def col_tile(w, c0):
            return w[:, bass.ds(c0, P)].rearrange("(k p) n -> p k n", p=P)

        def dst_cols(slot, tile=None):
            return (wraw if tile is None else tile)[:, slot, :].rearrange("p (k n) -> p k n", k=KD)

        def load_tile(sp, n, half, slot, src, first=False):
            if not first:
                sp.wait_ge(w_split, n - 1)
            dst = dst_cols(slot) if len(src.shape) == 3 else wraw[:, slot, :]
            sp.dma_start(dst, src).then_inc(raw_loaded[slot], 16)

        def split_tile(pool, n, half, slot, used=None, hi=None, lo=None):
            hi, lo = (whi, wlo) if hi is None else (hi, lo)
            pool.wait_ge(raw_loaded[slot], half * 16 + 16)
            if used is not None:
                pool.wait_ge(*used)
            pool.tensor_tensor(dst_cols(slot, hi), dst_cols(slot), ones[:, :].unsqueeze(1).to_broadcast([P, KD, P]),
                               ALU.mult).then_inc(w_hi, 1)
            pool.wait_ge(w_hi, n + 1)
            pool.tensor_tensor(lo[:, slot, :], wraw[:, slot, :], hi[:, slot, :].bitcast(F32),
                               ALU.subtract).then_inc(w_split, 1)

        def products(pe, out, w1, w2, r1, r2, start, stop):
            pe.matmul(out, w1, r1, start=start, stop=False)
            pe.matmul(out, w1, r2, start=False, stop=False)
            return pe.matmul(out, w2, r1, start=False, stop=stop)

        def gemm_tile(pe, n, q, slot, ready=None, free=True, hh=None, hl=None):
            hh, hl = (hhi, hlo) if hh is None else (hh, hl)
            pe.wait_ge(w_split, n + 1)
            for c, (o, w) in enumerate(CH):
                if ready is not None:
                    pe.wait_ge(ready[0], ready[1] + c + 1)
                if free:
                    pe.wait_ge(gemm_evac[slot], 3 * (q - 1) + c + 1)
                for k in range(KD):
                    mm = products(pe, SETS[slot][:, c, 0:w], whi[:, slot, bass.ts(k, P)],
                                  wlo[:, slot, bass.ts(k, P)], hh[:, k, o:o + w], hl[:, k, o:o + w],
                                  k == 0, k == KD - 1)
                mm.then_inc(gemm_done[slot], 1)

        def pool_consts(pool, ch):
            for t, val in ((ident, 0.0), (ones, 1.0), (blk, 0.0), (tri, 1.0), (delta8, 0.0), (hm, 0.0), (rep, 1.0),
                           (eps, EPS)):
                ch.run(pool.memset(t[tuple(slice(None) for _ in t.shape)], val))
            ch.run(pool.iota(piota[:, :], pattern=[[0, 1]], base=0, channel_multiplier=1))
            ch.run(pool.affine_select(out=ident[:, :], in_=ident[:, :], compare_op=ALU.not_equal, fill=1.0,
                                       base=0, pattern=[[-1, P]], channel_multiplier=1))
            for h in range(2):
                ch.run(pool.memset(blk[h * HD:(h + 1) * HD, h * HD:(h + 1) * HD], 1.0))
                ch.run(pool.memset(hm[h * HD:(h + 1) * HD, h:h + 1], 1.0))
            ch.run(pool.affine_select(out=tri[:, :], in_=tri[:, :], compare_op=ALU.is_ge, fill=0.0,
                                       base=0, pattern=[[1, P]], channel_multiplier=-1))
            ch.run(pool.affine_select(out=delta8[:, :, :], in_=delta8[:, :, :], compare_op=ALU.not_equal, fill=1.0,
                                       base=0, pattern=[[1, NS], [-1, NS]], channel_multiplier=0))
            ch.run(pool.affine_select(out=rep[:, :], in_=rep[:, :], compare_op=ALU.is_ge, fill=0.0,
                                       base=0, pattern=[[1, P]], channel_multiplier=-NH))
            ch.run(pool.affine_select(out=rep[:, :], in_=rep[:, :], compare_op=ALU.is_ge, fill=0.0,
                                       base=NH - 1, pattern=[[-1, P]], channel_multiplier=NH))
            pool.memset(top8[:, :], 0.0).then_inc(const_ready, 1)

        PARAMS = []
        for t, name in ((g1, "g_ffn1"), (gm, "g_mix"), (g2, "g_ffn2")):
            PARAMS.append((t[:, :], A[name][0].rearrange("(k p) -> p k", p=P)))
        for h in range(2):
            hs = slice(h * HD, (h + 1) * HD)
            PARAMS.append((gq[hs, :], A["g_q"][0].rearrange("(p a) -> p a", a=1)))
            PARAMS.append((gk[hs, :], A["g_k"][0].rearrange("(p a) -> p a", a=1)))
            PARAMS.append((dsk[hs, :], A["d_skip"][0].rearrange("(k h) -> h k", h=2)[h].partition_broadcast(HD)))
        for j in range(4):
            PARAMS.append((cw[:, :, j], A["conv_w"][0, j].rearrange("(k p) -> p k", p=P)))
        PARAMS.append((cb[:, :], A["conv_b"][0].rearrange("(k p) -> p k", p=P)))
        PARAMS.append((gssd[:, :], A["g_ssd_norm"][0].rearrange("(k p) -> p k", p=P)))
        PARAMS.append((dtb[:, :], A["dt_bias"][0].rearrange("(p a) -> p a", a=1)))
        PARAMS.append((nega[:, :], A["a_log"][0].rearrange("(p a) -> p a", a=1)))
        PARAMS.append((ptab[:, :], A["page_table"].rearrange("b n -> (b n)").partition_broadcast(P)))
        N_PARAMS = len(PARAMS)

        def act_params(act):
            for dst, src in PARAMS:
                act.dma_start(dst, src).then_inc(params_loaded, 16)

        NORMG = [g1, gm, g2]

        def act_norm(act, r):
            for c, (o, w) in enumerate(CH):
                if c:
                    act.wait_ge(ss_done, 3 * r + c)
                act.activation(sq[:, :, 0:w], X[:, :, o:o + w], ACT.Square).then_inc(sq_done, 1)
                act.wait_ge(ss_done, 3 * r + c + 1)
                act.activation(rt[:, c, 0:w], CD[c % 2][:, 0:w], ACT.Sqrt, bias=eps[:, 0:1],
                               scale=1.0 / D).then_inc(rt_done, 1)

        def pe_norm(pe, r):
            for c, (o, w) in enumerate(CH):
                pe.wait_ge(sq_done, 3 * r + c + 1)
                if c == 2:
                    pe.wait_ge(rt_done, 3 * r + 1)
                for k in range(KD):
                    mm = pe.matmul(CD[c % 2][:, 0:w], ones[:, :], sq[:, k, 0:w], start=k == 0, stop=k == KD - 1)
                mm.then_inc(ss_done, 1)

        def dve_norm(v, r, ch):
            for c, (o, w) in enumerate(CH):
                v.wait_ge(rt_done, 3 * r + c + 1)
                ch.step(v.reciprocal(rs[:, c, 0:w], rt[:, c, 0:w]))
                ch.settle()
                for k in range(KD):
                    ch.step(v.scalar_tensor_tensor(hf[:, k, 0:w], X[:, k, o:o + w], NORMG[r][:, k:k + 1],
                                                   rs[:, c, 0:w], ALU.mult, ALU.mult))
                ch.settle()
                ch.step(v.tensor_copy(hhi[:, :, o:o + w], hf[:, :, 0:w]))
                ch.settle()
                v.tensor_tensor(hlo[:, :, o:o + w], hf[:, :, 0:w], hhi[:, :, o:o + w].bitcast(F32),
                                ALU.subtract).then_inc(h_ready, 1)
            v.wait_ge(h_ready, 3 * r + 3)

        NI = NF // 2

        def ffn_tiles(f):
            g, u, d = (A["w_ffn1_gate"], A["w_ffn1_up"], A["w_ffn1_down"]) if f == 0 else \
                      (A["w_ffn2_gate"], A["w_ffn2_up"], A["w_ffn2_down"])
            return g[0], u[0], d[0]

        def sp_ffn(sp, f):
            g, u, d = ffn_tiles(f)
            n0 = TILE_FFN1 if f == 0 else TILE_FFN2
            for j in range(4):
                load_tile(sp, n0 + j, 0, j % 2, col_tile([g, u][j % 2], (j // 2) * P), first=n0 + j < 2)
            with sp.Fori(0, NI - 1) as i:
                n = n0 + 4 + i * 6
                load_tile(sp, n, 0, 0, col_tile(g, i * 256 + 256))
                load_tile(sp, n + 1, 0, 1, col_tile(u, i * 256 + 256))
                load_tile(sp, n + 2, 0, 0, d[bass.ds(i * 256, P), :])
                load_tile(sp, n + 3, 0, 1, d[bass.ds(i * 256 + P, P), :])
                load_tile(sp, n + 4, 0, 0, col_tile(g, i * 256 + 384))
                load_tile(sp, n + 5, 0, 1, col_tile(u, i * 256 + 384))
            n = n0 + FFN_TILES - 2
            load_tile(sp, n, 0, 0, d[DFF - 256:DFF - 128, :])
            load_tile(sp, n + 1, 0, 1, d[DFF - 128:DFF, :])

        def raw_count(n):
            if n < TILE_IN + 8:
                return n // 2
            if n < TILE_IN + 16:
                return n // 2 + (n - TILE_IN - 8) // 2 + 1
            if n < TILE_AO:
                return n // 2 + 4
            if n < TILE_SO:
                return n // 2 + 4 + 3 * ((n - TILE_AO) // 2)
            return n // 2 + 16

        def pool_ffn(pool, f):
            n0, q0 = (TILE_FFN1, ORD_FFN1) if f == 0 else (TILE_FFN2, ORD_FFN2)
            for j in range(4):
                q = q0 + j // 2
                split_tile(pool, n0 + j, raw_count(n0 + j), j % 2, (gemm_done[j % 2], 3 * q) if q else None)
            pool.wait_ge(h_ready, 3 * (0 if f == 0 else 2) + 3)
            with pool.Fori(0, NI - 1) as i:
                for j in range(6):
                    slot = j % 2
                    prev = [(gemm_done[slot], i * 6 + 3 * (q0 + 2)), (gemm_done[0], i * 6 + (3 * (q0 + 1) + 1)),
                            (gemm_done[slot], i * 6 + 3 * (q0 + 3))][j // 2]
                    parts = (whid, wlod) if j // 2 == 1 else (None, None)
                    split_tile(pool, i * 6 + (n0 + 4 + j), i * 3 + raw_count(n0 + 4 + j), slot, prev, *parts)
            n = n0 + FFN_TILES - 2
            for j in range(2):
                split_tile(pool, n + j, raw_count(n + j), j, (gemm_done[0], 6 * (NI - 1) + 3 * (q0 + 1) + 1), whid, wlod)

        def pe_down(pe, f, n, i, last_ready):
            pe.wait_ge(w_split, n + 2)
            pe.wait_ge(hid_ready, last_ready)
            for m in range(KD):
                for c, (o, w) in enumerate(CH):
                    u = 3 * m + c
                    if u >= 2:
                        pe.wait_ge(down_evac, i * 24 + (f * 24 * NI + u - 1))
                    for j in range(2):
                        mm = products(pe, CD[u % 2][:, 0:w], whid[:, j, bass.ts(m, P)], wlod[:, j, bass.ts(m, P)],
                                      hidhi[:, j, o:o + w], hidlo[:, j, o:o + w], j == 0, j == 1)
                    mm.then_inc(down_done, 1)

        def pe_ffn(pe, f):
            n0, q0, r = (TILE_FFN1, ORD_FFN1, 0) if f == 0 else (TILE_FFN2, ORD_FFN2, 2)
            for j in range(4):
                gemm_tile(pe, n0 + j, q0 + j // 2, j % 2, ready=(h_ready, 3 * r) if j == 0 else None,
                               free=q0 + j // 2 > 0)
            with pe.Fori(0, NI - 1) as i:
                n, q = n0 + 4 + i * 6, q0 + 2 + i * 2
                for j in range(2):
                    gemm_tile(pe, n + j, q, j)
                pe_down(pe, f, n + 2, i, i * 6 + (f * 3 * NF + 6))
                for j in range(2):
                    gemm_tile(pe, n + 4 + j, q + 1, j)
            pe_down(pe, f, n0 + FFN_TILES - 2, NI - 1, (f + 1) * 3 * NF)

        def act_gate(act, f, q, k):
            for c, (o, w) in enumerate(CH):
                act.wait_ge(gemm_done[0], q * 3 + c + 1)
                if not isinstance(k, int) or k > 0:
                    act.wait_ge(hid_mult, (k - 1) * 3 + (f * 3 * NF + c + 1))
                act.activation(sg[:, o:o + w], setA[:, c, 0:w], ACT.Silu).then_inc(gemm_evac[0], 1)

        def act_ffn(act, f):
            q0 = ORD_FFN1 if f == 0 else ORD_FFN2
            for k in range(2):
                act_gate(act, f, q0 + k, k)
            with act.Fori(0, NI - 1) as i:
                for k in range(2):
                    act_gate(act, f, q0 + 2 + k + i * 2, i * 2 + (2 + k))

        def dve_hidden(v, f, q, k, j, hch):
            for c, (o, w) in enumerate(CH):
                v.wait_ge(gemm_done[1], q * 3 + c + 1)
                v.wait_ge(gemm_evac[0], q * 3 + c + 1)
                v.tensor_tensor(hidf[:, o:o + w], sg[:, o:o + w], setB[:, c, 0:w], ALU.mult)\
                    .then_inc(hid_mult, 1)
                v.wait_ge(hid_mult, k * 3 + (f * 3 * NF + c + 1))
                v.tensor_copy(hidhi[:, j, o:o + w], hidf[:, o:o + w]).then_inc(gemm_evac[1], 1)
                v.wait_ge(gemm_evac[1], q * 3 + c + 1)
                v.tensor_tensor(hidlo[:, j, o:o + w], hidf[:, o:o + w], hidhi[:, j, o:o + w].bitcast(F32),
                                ALU.subtract).then_inc(hid_ready, 1)

        def dve_down(v, f, i):
            for m in range(KD):
                for c, (o, w) in enumerate(CH):
                    u = 3 * m + c
                    v.wait_ge(down_done, i * 24 + (f * 24 * NI + u + 1))
                    v.scalar_tensor_tensor(X[:, m, o:o + w], CD[u % 2][:, 0:w], 0.5, X[:, m, o:o + w],
                                           ALU.mult, ALU.add).then_inc(down_evac, 1)

        def dve_ffn(v, f):
            q0 = ORD_FFN1 if f == 0 else ORD_FFN2
            for k in range(2):
                dve_hidden(v, f, q0 + k, k, k, None)
            with v.Fori(0, NI - 1) as i:
                dve_down(v, f, i)
                for k in range(2):
                    dve_hidden(v, f, q0 + 2 + k + i * 2, i * 2 + (2 + k), k, None)
            dve_down(v, f, NI - 1)
            v.wait_ge(down_evac, f * 24 * NI + 24 * NI)


        w_in = A["w_in"][0]
        nsq_done, nss_done, nrt_done, qk_ready = (sem(n) for n in ("nsq_done", "nss_done", "nrt_done", "qk_ready"))
        tok_done, tok_evac, kit_stored = (sem(n) for n in ("tok_done", "tok_evac", "kit_stored"))
        idx_done, idx_relu, idx_acc, sc_masked, mb_ready = (
            sem(n) for n in ("idx_done", "idx_relu", "idx_acc", "sc_masked", "mb_ready"))
        topk_step = sem("topk_step")
        spill_out = [sem("spill_out0"), sem("spill_out1")]
        conv_done, conv_silu = sem("conv_done"), sem("conv_silu")
        conv_out = [sem("conv_out0"), sem("conv_out1")]
        conv_step = sem("conv_step")

        def flat(t, k=None):
            return t[:, :] if k is None else t[:, k, :]
        HEADS = [(kiwi, None), (dtT, None), (qiT, 0), (qiT, 1), (vT, 0), (vT, 1), (kT, 0), (kT, 1)] + \
                [(qT, j) for j in range(KD)]
        NORM_UNITS = [(t, k, c) for t, k in HEADS[6:] for c in range(3)]
        IDX_UNITS = [(t, h) for t in range(2, NT) for h in range(4)]
        QROWS = [P] * (NT - 1) + [LAST]

        def head_src(j):
            if j < 8:
                return [COL["kiwi"], COL["dt"], COL["qi"], COL["qi"] + P, COL["v"], COL["v"] + P,
                        COL["k"], COL["k"] + P][j]
            c, g = (j - 8) // 4, (j - 8) % 4
            return (8 * c + g) * HD, (8 * c + 4 + g) * HD

        def sp_in(sp):
            n = TILE_IN
            for j in range(16):
                src = head_src(j)
                if isinstance(src, int):
                    load_tile(sp, n + j, 0, j % 2, col_tile(w_in, src))
                else:
                    sp.wait_ge(w_split, n + j - 1)
                    for half in range(2):
                        sp.dma_start(dst_cols(j % 2)[:, :, half * HD:(half + 1) * HD],
                                     w_in[:, src[half]:src[half] + HD].rearrange("(k p) n -> p k n", p=P))\
                            .then_inc(raw_loaded[j % 2], 16)
            for off, c0, pairs in ((16, COL["z"], 8), (32, COL["ga"], 4), (40, COL["gs"], 4), (48, COL["xbc"], 12)):
                with sp.Fori(0, pairs) as i:
                    for j in range(2):
                        load_tile(sp, i * 2 + (n + off + j), 0, j, col_tile(w_in, i * 256 + (c0 + j * P)))

        def pool_in(pool, ch):
            for j in range(16):
                n = TILE_IN + j
                prev = (gemm_done[j % 2], 3 * (ORD_IN + j // 2))
                split_tile(pool, n, raw_count(n), j % 2, prev)
            for j in range(2):
                split_tile(pool, TILE_IN + 16 + j, raw_count(TILE_IN + 16), j, (gemm_done[j], 3 * (ORD_IN + 8)))
            pool.wait_ge(kit_stored, 32)
            pool.wait_ge(tok_evac, NT + 2)
            for t in range(2):
                m = mb[:, MOFF[t]:MOFF[t] + WID[t]]
                ch.run(pool.memset(m, 0.0))
                ch.run(pool.affine_select(out=m, in_=m, compare_op=ALU.is_ge, fill=MASKED, base=t * P,
                                          pattern=[[-1, WID[t]]], channel_multiplier=1))
            for t in range(2, NT):
                pool.wait_ge(idx_acc, 4 * (t - 1))
                o, w = SOFF[t] + t * P, WID[t] - t * P
                m = sc[0:QROWS[t], o:o + w]
                pool.affine_select(out=m, in_=m, compare_op=ALU.is_ge, fill=MASKED, base=0,
                                   pattern=[[-1, w]], channel_multiplier=1).then_inc(sc_masked, 1)
            pool_rest(pool, TILE_IN + 18, ORD_IN + 9, (N_IN - 18) // 2)

        def pool_rest(pool, n0, q0, pairs):
            with pool.Fori(0, pairs) as i:
                for j in range(2):
                    split_tile(pool, i * 2 + (n0 + j), i + raw_count(n0 + 0) , j, (gemm_done[j], i * 3 + 3 * q0))

        def pe_in(pe):
            pe_norm(pe, 1)
            for j in range(16):
                gemm_tile(pe, TILE_IN + j, ORD_IN + j // 2, j % 2, ready=(h_ready, 3) if j == 0 else None)
            pe.wait_ge(gemm_evac[0], 3 * (ORD_IN + 8))
            pe.wait_ge(gemm_evac[1], 3 * (ORD_IN + 8))
            for t in range(NT + 1):
                o, w = (t * P, QROWS[t]) if t < NT else (L, NS)
                if t >= 2:
                    pe.wait_ge(tok_evac, t - 1)
                pe.transpose(CD[t % 2][0:w, 0:68], kiwi[0:68, o:o + w], ident[0:68, 0:68])
                for k in range(2):
                    mm = pe.transpose(CD[t % 2][0:w, P + k * P:2 * P + k * P], vT[:, k, o:o + w], ident[:, :])
                mm.then_inc(tok_done, 1)
            pe.wait_ge(tok_evac, NT + 1)
            for u, (src, k, c) in enumerate(NORM_UNITS):
                o, w = CH[c]
                pe.wait_ge(nsq_done, u + 1)
                if u >= 2:
                    pe.wait_ge(nrt_done, u - 1)
                pe.matmul(CD[u % 2][:, 0:w], blk[:, :], nsq[:, u % 2, 0:w], start=True, stop=True).then_inc(nss_done, 1)
            pe.wait_ge(tok_evac, NT + 2)
            for u, (t, h) in enumerate(IDX_UNITS):
                if u >= 2:
                    pe.wait_ge(idx_relu, u - 1)
                hs = slice((h % 2) * HD, (h % 2) * HD + HD)
                qn = QROWS[t]
                for j in range((WID[t] + 511) // 512):
                    n = min(512, WID[t] - 512 * j)
                    mm = pe.matmul(SETS[u % 2][0:qn, j, 0:n], qiT[hs, h // 2, t * P:t * P + qn],
                                   ki2[hs, 512 * j:512 * j + n], start=True, stop=True)
                mm.then_inc(idx_done, 1)
            pe.wait_ge(idx_relu, len(IDX_UNITS))
            with pe.Fori(0, (N_IN - 16) // 2) as i:
                for j in range(2):
                    gemm_tile(pe, i * 2 + (TILE_IN + 16 + j), i + (ORD_IN + 8), j)

        def act_in(act):
            act.wait_ge(down_evac, 24 * NI)
            act.dma_start(xD.rearrange("(k p) t -> p k t", p=P), X[:, :, :]).then_inc(x_spilled, 16)
            act_norm(act, 1)
            act.wait_ge(x_spilled, 16)
            for j, (dst, k) in enumerate(HEADS):
                rows = SH if dst is dtT else P
                for c, (o, w) in enumerate(CH):
                    act.wait_ge(gemm_done[j % 2], 3 * (ORD_IN + j // 2) + c + 1)
                    act.activation(flat(dst, k)[0:rows, o:o + w], SETS[j % 2][0:rows, c, 0:w], ACT.Identity)\
                        .then_inc(gemm_evac[j % 2], 1)
            act.wait_ge(tok_evac, NT + 1)
            full = (NT - 1) * P

            def token_stores(dst, src, f):
                yield dst[0:full, :].rearrange("(t p) f -> p t f", p=P), src[:, 0:NT - 1, 0:f]
                yield dst[full:L, :], src[0:LAST, NT - 1, 0:f]
            for d, s_ in token_stores(O["kidx_prompt"][0, 0], kit, HD):
                act.dma_start(d, s_).then_inc(kit_stored, 16)
            for d, s_ in token_stores(O["v_prompt"][0, 0].rearrange("t h d -> t (h d)"), vtok, 256):
                store(act, d, s_)
            store(act, O["kidx_sample"].rearrange("l b s d -> (l b s) d"), kis[:, 0:HD])
            store(act, O["v_sample"].rearrange("l b s h d -> (l b s) (h d)"), vsam[:, :])

            def square(u):
                src, k, c = NORM_UNITS[u]
                o, w = CH[c]
                if u >= 2:
                    act.wait_ge(nss_done, u - 1)
                act.activation(nsq[:, u % 2, 0:w], src[:, k, o:o + w], ACT.Square).then_inc(nsq_done, 1)
            square(0)
            for u, (src, k, c) in enumerate(NORM_UNITS):
                if u + 1 < len(NORM_UNITS):
                    square(u + 1)
                w = CH[c][1]
                act.wait_ge(nss_done, u + 1)
                if u >= 2:
                    act.wait_ge(qk_ready, u - 1)
                act.activation(nrt[:, u % 2, 0:w], CD[u % 2][:, 0:w], ACT.Sqrt, bias=eps[:, 0:1],
                               scale=1.0 / HD).then_inc(nrt_done, 1)
            for u, (t, h) in enumerate(IDX_UNITS):
                act.wait_ge(idx_done, u + 1)
                if u >= 2:
                    act.wait_ge(idx_acc, u - 1)
                qn = QROWS[t]
                act.activation(relu[0:qn, u % 2, 0:WID[t]],
                               SETS[u % 2][0:qn, :, :].rearrange("p a b -> p (a b)")[:, 0:WID[t]], ACT.Relu)\
                    .then_inc(idx_relu, 1)
            act.wait_ge(idx_acc, len(IDX_UNITS))
            q = ORD_IN + 8
            for dst, pairs, func, m0 in ((zD, 8, ACT.Silu, 0), (gaD, 4, ACT.Sigmoid, 8), (gsD, 4, ACT.Sigmoid, 12)):
                start = 0
                if m0 == 0:
                    spill_tile_pair(act, dst, func, q, 0, 0, True)
                    start = 1
                with act.Fori(start, pairs) as i:
                    spill_tile_pair(act, dst, func, i + (q + m0), i + m0, i, False)
            q = ORD_IN + 24

            def raw(i, j, first):
                if not first:
                    act.wait_ge(conv_done, i * 2 + (j - 1))
                for c, (o, w) in enumerate(CH):
                    act.wait_ge(gemm_done[j], i * 3 + (3 * q + c + 1))
                    act.activation(xraw[:, j, 4 + o:4 + o + w], SETS[j][:, c, 0:w], ACT.Identity)\
                        .then_inc(gemm_evac[j], 1)

            def out(i, j):
                act.wait_ge(conv_done, i * 2 + (j + 1))
                act.activation(cv[:, j, 0:L], cv[:, j, 0:L], ACT.Silu).then_inc(conv_silu, 1)
                act.wait_ge(conv_silu, i * 2 + (j + 1))
                act.dma_start(xcD[bass.ds(i * 256 + j * P, P), 0:L], cv[:, j, 0:L]).then_inc(conv_out[j], 16)
            raw(0, 0, True)
            raw(0, 1, True)
            out(0, 0)
            with act.Fori(1, 12) as i:
                raw(i, 0, False)
                out(i - 1, 1)
                raw(i, 1, False)
                out(i, 0)
            out(11, 1)

        def spill_tile_pair(act, dst, func, q, m, i, first):
            for j in range(2):
                if not first:
                    act.wait_ge(spill_out[j], m * 16)
                for c, (o, w) in enumerate(CH):
                    act.wait_ge(gemm_done[j], q * 3 + c + 1)
                    act.activation(spill[:, j, o:o + w], SETS[j][:, c, 0:w], func).then_inc(gemm_evac[j], 1)
                act.wait_ge(gemm_evac[j], q * 3 + 3)
                act.dma_start(dst[bass.ds(i * 256 + j * P, P), :], spill[:, j, :]).then_inc(spill_out[j], 16)

        def dve_in(v, ch):
            dve_norm(v, 1, ch)
            for t in range(NT + 1):
                w = QROWS[t] if t < NT else NS
                v.wait_ge(tok_done, t + 1)
                kd = kit[0:w, t, :] if t < NT else kis[:, :]
                vd = vtok[0:w, t, :] if t < NT else vsam[:, :]
                v.tensor_copy(kd, CD[t % 2][0:w, 0:68])
                v.tensor_copy(vd, CD[t % 2][0:w, P:3 * P]).then_inc(tok_evac, 1)
            v.tensor_copy(ki2[0:HD, :], kiwi[0:HD, :])
            v.tensor_copy(ki2[HD:P, :], kiwi[0:HD, :])
            v.tensor_copy(kxs[0:HD, :], kiwi[0:HD, L:T])
            v.tensor_copy(kxs[HD:P, :], kiwi[0:HD, L:T])
            v.tensor_copy(qis[:, :, :], qiT[:, :, L:T])
            v.wait_ge(tok_evac, NT + 1)
            WSC = (HD ** -0.5) * (4 ** -0.5)
            ch.step(v.tensor_scalar(wi9[:, 0:NT - 1, :], kit[:, 0:NT - 1, HD:68], WSC, None, ALU.mult))
            v.tensor_scalar(wi9[0:LAST, NT - 1, :], kit[0:LAST, NT - 1, HD:68], WSC, None, ALU.mult)\
                .then_inc(tok_evac, 1)
            for u, (src, k, c) in enumerate(NORM_UNITS):
                o, w = CH[c]
                v.wait_ge(nrt_done, u + 1)
                if u:
                    v.wait_ge(qk_ready, u)
                ch.run(v.reciprocal(nrs[:, 0:w], nrt[:, u % 2, 0:w]))
                g = gk if src is kT else gq
                v.scalar_tensor_tensor(src[:, k, o:o + w], src[:, k, o:o + w], g[:, 0:1], nrs[:, 0:w],
                                       ALU.mult, ALU.mult).then_inc(qk_ready, 1)
            v.wait_ge(qk_ready, len(NORM_UNITS))
            v.wait_ge(tok_evac, NT + 2)
            for u, (t, h) in enumerate(IDX_UNITS):
                qn, w = QROWS[t], WID[t]
                v.wait_ge(idx_relu, u + 1)
                dst = sc[0:qn, SOFF[t]:SOFF[t] + w]
                if h == 0:
                    v.tensor_scalar(dst, relu[0:qn, u % 2, 0:w], wi9[0:qn, t, 0:1], None, ALU.mult).then_inc(idx_acc, 1)
                else:
                    v.wait_ge(idx_acc, u)
                    v.scalar_tensor_tensor(dst, relu[0:qn, u % 2, 0:w], wi9[0:qn, t, h:h + 1], dst,
                                           ALU.mult, ALU.add).then_inc(idx_acc, 1)
            v.wait_ge(kit_stored, 32)
            rounds = TOPK // 8

            def rounds_of(t, n, first):
                s_ = sc[0:QROWS[t], SOFF[t]:SOFF[t] + WID[t]]
                t8 = top8[0:QROWS[t], :]
                for k in range(n):
                    v.max(t8, s_).then_inc(topk_step, 1)
                    v.wait_ge(topk_step, first * 2 + (2 * k + 1))
                    v.tensor_copy(held[0:QROWS[t], :], t8[:, 0:1])
                    v.match_replace(s_, t8, s_, TAKEN).then_inc(topk_step, 1)
                    v.wait_ge(topk_step, first * 2 + (2 * k + 2))
                    v.tensor_copy(held2[0:QROWS[t], :], ones[0:QROWS[t], 0:1])

            def bias_of(t):
                qn, w = QROWS[t], WID[t]
                v.tensor_scalar(mb[0:qn, MOFF[t]:MOFF[t] + w], sc[0:qn, SOFF[t]:SOFF[t] + w], TAKEN * 0.5, MASKED,
                                ALU.is_gt, ALU.mult).then_inc(mb_ready, 1)
            v.wait_ge(sc_masked, NT - 2)
            LATE = (NT - 4, NT - 3, NT - 2)
            EARLY = [t for t in range(2, NT) if t not in LATE]
            CONV_STEPS = CONVD // P // 2 - 1
            early_rounds = rounds - 2 * CONV_STEPS
            n = 0
            for tiles, count in ((EARLY, rounds), (LATE, early_rounds)):
                for t in tiles:
                    with v.Fori(0, count) as i:
                        rounds_of(t, 1, i + n)
                    n += count
                    if tiles is EARLY:
                        bias_of(t)
            ch.run(v.memset(xraw[:, :, 0:4], 0.0))
            q = ORD_IN + 24

            def conv(i, j, first):
                b = i * 2 + j
                v.wait_ge(gemm_evac[j], i * 3 + 3 * (q + 1))
                if not first:
                    v.wait_ge(conv_out[j], i * 16)
                n = (i * 2 + j) * 3
                out = cv[:, j, 0:L]
                v.tensor_scalar(out, xraw[:, j, 1:1 + L], cw[:, bass.ds(b, 1), 0], cb[:, bass.ds(b, 1)],
                                ALU.mult, ALU.add).then_inc(conv_step, 1)
                v.tensor_copy(rtail[:, bass.ds(b, 1), :], xraw[:, j:j + 1, 4 + T - 24:4 + T])
                for tap in range(1, 4):
                    v.wait_ge(conv_step, n + tap)
                    ins = v.scalar_tensor_tensor(out, xraw[:, j, 1 + tap:1 + tap + L], cw[:, bass.ds(b, 1), tap],
                                                 out, ALU.mult, ALU.add)
                    ins.then_inc(conv_step if tap < 3 else conv_done, 1)
            conv(0, 0, True)
            conv(0, 1, True)
            with v.Fori(1, 12) as i:
                for j in range(2):
                    conv(i, j, False)
                for k, t in enumerate(LATE):
                    rounds_of(t, 2, i * 6 + (n - 6 + 2 * k))
            for t in LATE:
                bias_of(t)
            v.wait_ge(mb_ready, NT - 2)
            v.wait_ge(conv_done, 24)


        over = [sem(f"phase_over{i}") for i in range(4)]

        def phase_over(eng, i):
            eng.drain().then_inc(over[i], 1)
            eng.wait_ge(over[i], 5)

        kt_done, kt_evac, pidx_ready, gathered, vflat_loaded = (
            sem(n) for n in ("kt_done", "kt_evac", "pidx_ready", "gathered", "vflat_loaded"))
        k_stored = sem("k_stored")
        s_done, s_masked, exp_done, o_done, o_evac, ot_done, ot_evac = (
            sem(n) for n in ("s_done", "s_masked", "exp_done", "o_done", "o_evac", "ot_done", "ot_evac"))
        pt_done = [sem("pt_doneC"), sem("pt_doneD")]
        pt_evac = [sem("pt_evacC"), sem("pt_evacD")]
        AU = [(t, pos) for t in range(NT) for pos in range(NH)]
        FULL = (NT - 1) * P

        def groups(t):
            nb = WID[t] // P
            g = [(0, 0, min(4, nb), P)]
            if nb > 4:
                g.append((1, 4, nb - 4, P))
            if WID[t] % P:
                g.append((1, nb, 1, WID[t] % P))
            return g
        DCOUNT = [0]
        for t, _ in AU:
            DCOUNT.append(DCOUNT[-1] + sum(b for b, *_ in groups(t)))

        s_idx, s_idx_e, s_row, s_row_e, s_pv = (sem(n) for n in ("smp_key_T", "smp_key_evac", "smp_row", "smp_row_evac", "smp_pv"))
        s_dots, s_relu, s_top, s_rdy = (sem(n) for n in ("smp_dots", "smp_relu", "smp_topk", "smp_ready"))
        s_kT, s_kTe = sem("smp_kT"), sem("smp_kT_evac")
        s_sc, s_exp, s_pT, s_pTe = (sem(n) for n in ("smp_scores", "smp_exp", "smp_pT", "smp_pT_evac"))

        def sp_attn(sp):
            phase_over(sp, 0)
            sp.wait_ge(kt_evac, NT + 1)
            kp = O["k_prompt"][0, 0].rearrange("t h d -> t (h d)")
            sp.dma_start(kp[0:FULL, :].rearrange("(t p) f -> p t f", p=P), kout[:, 0:NT - 1, :]).then_inc(k_stored, 16)
            sp.dma_start(kp[FULL:L, :], kout[0:LAST, NT - 1, :]).then_inc(k_stored, 16)
            store(sp, O["k_sample"].rearrange("l b s h d -> (l b s) (h d)"), ksam[:, :])
            sp.wait_ge(s_idx, NS)
            sp.dma_start(vflat[0:1, :, :], vsam[:, :]).then_inc(vflat_loaded, 16)
            sp.wait_ge(vflat_loaded, 16)
            phase_over(sp, 1)

        def pool_attn(pool, ch):
            phase_over(pool, 0)
            pool.wait_ge(pidx_ready, 2)
            for dst, cache, f in ((kg, "cache_k", 256), (vg, "cache_v", 256), (kidxg, "cache_kidx", HD)):
                src = A[cache][0]
                src = src.rearrange("n s h d -> (n s) (h d)") if f == 256 else src.rearrange("n s d -> (n s) d")
                if dst is kidxg:
                    pool.wait_ge(k_stored, 32)
                for i in range(NS * PAGES):
                    pool.indirect_dma_start(out=dst[:, i, :], out_offset=None, in_=src,
                                            in_offset=bass.IndirectOffsetOnAxis(ap=pidx[:, i:i + 1], axis=0))\
                        .then_inc(gathered, 16)
            pool.wait_ge(gathered, 16 * 3 * NS * PAGES)
            phase_over(pool, 1)

        def pe_attn(pe):
            phase_over(pe, 0)
            for t in range(NT + 1):
                o, w = (t * P, QROWS[t]) if t < NT else (L, NS)
                if t >= 2:
                    pe.wait_ge(kt_evac, t - 1)
                for k in range(2):
                    mm = pe.transpose(CD[t % 2][0:w, k * P:k * P + P], kT[:, k, o:o + w], ident[:, :])
                mm.then_inc(kt_done, 1)
            pe.wait_ge(kt_evac, NT + 1)

            def scores(u):
                t, pos = AU[u]
                qn, j, hs = QROWS[t], pos // 2, slice((pos % 2) * HD, (pos % 2) * HD + HD)
                if u >= 2 and WID[t] <= 1024:
                    pe.wait_ge(s_masked, u - 1)
                elif u >= 2:
                    pe.wait_ge(o_evac, u - 1)
                for i in range((WID[t] + 511) // 512):
                    n = min(512, WID[t] - 512 * i)
                    mm = pe.matmul(SETS[u % 2][0:qn, i, 0:n], qT[hs, j, t * P:t * P + qn],
                                   kT[hs, j // 4, 512 * i:512 * i + n], start=True, stop=True)
                mm.then_inc(s_done, 1)

            def transposes(u):
                t, pos = AU[u]
                qn = QROWS[t]
                pe.wait_ge(exp_done, u + 1)
                dn = DCOUNT[u]
                for bank, b0, nb, kn in groups(t):
                    before = u if bank == 0 else dn
                    if before:
                        pe.wait_ge(pt_evac[bank], before)
                    if pos == 0 and t > 0 and b0 in (0, 4):
                        pe.wait_ge(ot_evac, 2 * t)
                    for b in range(nb):
                        mm = pe.transpose(CD[bank][0:kn, b * P:b * P + qn],
                                          pr[0:qn, u % 2, (b0 + b) * P:(b0 + b) * P + kn], ident[0:qn, 0:qn])
                    mm.then_inc(pt_done[bank], 1)
                    dn += bank

            def values(u):
                t, pos = AU[u]
                qn, kv = QROWS[t], 2 * (pos // 8) + pos % 2
                pe.wait_ge(pt_evac[0], u + 1)
                if DCOUNT[u + 1]:
                    pe.wait_ge(pt_evac[1], DCOUNT[u + 1])
                if u >= 2:
                    pe.wait_ge(o_evac, u - 1)
                nb = (WID[t] + P - 1) // P
                for b in range(nb):
                    kn = min(P, WID[t] - b * P)
                    mm = pe.matmul(SETS[u % 2][0:qn, 2, 256:256 + HD], ptT[0:kn, u % 2, b, 0:qn],
                                   vtok[0:kn, b, kv * HD:(kv + 1) * HD], start=b == 0, stop=b == nb - 1)
                mm.then_inc(o_done, 1)

            def outputs(t):
                qn = QROWS[t]
                pe.wait_ge(o_evac, NH * (t + 1))
                for half in range(2):
                    for k in range(4):
                        mm = pe.transpose(CD[half][:, k * P:k * P + qn],
                                          otok[0:qn, t % 2, (4 * half + k) * P:(4 * half + k + 1) * P], ident[0:qn, 0:qn])
                    mm.then_inc(ot_done, 1)
            scores(0)
            for u, (t, pos) in enumerate(AU):
                wide = u + 1 < len(AU) and WID[AU[u + 1][0]] > 1024
                if pos and wide:
                    values(u - 1)
                if u + 1 < len(AU):
                    scores(u + 1)
                transposes(u)
                if pos and not wide:
                    values(u - 1)
                if pos == NH - 1:
                    values(u)
                    outputs(t)
            pe.wait_ge(ot_evac, 2 * NT)
            SC = [setA[:, 0, :], setA[:, 1, :], setB[:, 0, :], setB[:, 1, :]]
            pe.wait_ge(gathered, 16 * 3 * NS * PAGES)
            pe.wait_ge(s_rdy, 1)
            for b in range(NS + 1):
                if b < NS:
                    if b >= 2:
                        pe.wait_ge(s_idx_e, b - 1)
                    for pg in range(PAGES):
                        mm = pe.transpose(CD[b % 2][0:HD, pg * P:(pg + 1) * P], kidxg[:, b * PAGES + pg, :], ident[:, :])
                    mm.then_inc(s_idx, 1)
                if b >= 1:
                    a_ = b - 1
                    pe.wait_ge(s_idx_e, b)
                    for h in range(4):
                        hs = slice((h % 2) * HD, (h % 2) * HD + HD)
                        mm = pe.matmul(SC[h][0:NS, :], qz[hs, h // 2, a_, :], kxT[hs, a_ % 2, :],
                                       start=a_ == 0, stop=a_ == NS - 1)
                    mm.then_inc(s_dots, 1)
            for h in range(4):
                hs = slice((h % 2) * HD, (h % 2) * HD + HD)
                mm = pe.matmul(SETS[h % 2][0:NS, 2, h * NS:(h + 1) * NS], qis[hs, h // 2, :], kxs[hs, :], start=True, stop=True)
            mm.then_inc(s_dots, 1)
            pe.wait_ge(s_top, 1)
            pe.wait_ge(s_rdy, 2)
            pe.matmul(setB[:, 0, :], rep[:, :], mss[:, 0:PAST], start=True, stop=False)
            pe.matmul(setB[:, 1, 0:1], rep[:, :], mss[:, PAST:PAST + 1], start=True, stop=False)
            for u in range(2 * NS + 1):
                if u < 2 * NS:
                    b, c = u // 2, u % 2
                    if u >= 2:
                        pe.wait_ge(s_kTe, u - 1)
                    for pg in range(PAGES):
                        mm = pe.transpose(CD[u % 2][:, pg * P:(pg + 1) * P], kg[:, b * PAGES + pg, c * P:(c + 1) * P],
                                          ident[:, :])
                    mm.then_inc(s_kT, 1)
                if u >= 1:
                    b, c = (u - 1) // 2, (u - 1) % 2
                    last = u == 2 * NS
                    pe.wait_ge(s_kTe, u)
                    pe.matmul(setB[:, 1, 0:1], qzz[:, u - 1, :], kT[:, c, L + b:L + b + 1], start=False, stop=last)
                    pe.matmul(setB[:, 0, :], qzz[:, u - 1, :], kgT[:, b % 2, c, :], start=False, stop=last)\
                        .then_inc(s_sc, 1)
            pe.wait_ge(s_exp, 1)
            for pg in range(PAGES):
                mm = pe.transpose(bankC[:, pg * P:(pg + 1) * P], ps_[:, pg * P:(pg + 1) * P], ident[:, :])
            mm.then_inc(s_pT, 1)
            pe.transpose(bankD[0:1, 0:P], ps_[:, PAST:PAST + 1], ident[:, :]).then_inc(s_pT, 1)
            pe.wait_ge(s_pTe, 2)
            pe.wait_ge(vflat_loaded, 16)
            for b in range(NS):
                for c in range(2):
                    rows = slice(b * NH + c * 8, b * NH + c * 8 + 8)
                    for pg in range(PAGES):
                        pe.matmul(setA[:, 0, rows], vg[:, b * PAGES + pg, c * P:(c + 1) * P], ptS[:, pg, rows],
                                  start=pg == 0, stop=False)
                    mm = pe.matmul(setA[:, 0, rows], vflat[0:1, b, c * P:(c + 1) * P], pnT[0:1, rows],
                                   start=False, stop=True)
            mm.then_inc(s_pv, 1)
            phase_over(pe, 1)

        def act_attn(act):
            act.wait_ge(conv_out[0], 16 * 12)
            act.wait_ge(conv_out[1], 16 * 12)
            act.wait_ge(spill_out[0], 16 * 16)
            act.wait_ge(spill_out[1], 16 * 16)
            phase_over(act, 0)
            for t in range(NT + 1):
                w = QROWS[t] if t < NT else NS
                act.wait_ge(kt_done, t + 1)
                dst = kout[0:w, t, :] if t < NT else ksam[:, :]
                act.activation(dst, CD[t % 2][0:w, 0:256], ACT.Identity).then_inc(kt_evac, 1)
            for u, (t, pos) in enumerate(AU):
                qn, w = QROWS[t], WID[t]
                act.wait_ge(s_masked, u + 1)
                if u >= 2:
                    act.wait_ge(o_done, u - 1)
                    act.wait_ge(o_evac, u - 1)
                act.activation(pr[0:qn, u % 2, 0:w], smx[0:qn, u % 2, 0:w], ACT.Exp, bias=nmax[0:qn, u % 2:u % 2 + 1],
                               scale=-1.0, accum_out=lsum[0:qn, u % 2:u % 2 + 1]).then_inc(exp_done, 1)
                _, b0, nb, kn = groups(t)[0]
                act.wait_ge(pt_done[0], u + 1)
                act.activation(ptT[:, u % 2, 0:nb, 0:qn],
                               bankC[:, 0:nb * P].rearrange("p (b q) -> p b q", q=P)[:, :, 0:qn], ACT.Identity)\
                    .then_inc(pt_evac[0], 1)
                if pos == NH - 1:
                    for half in range(2):
                        act.wait_ge(ot_done, 2 * t + half + 1)
                        act.activation(qT[:, 4 * half:4 * half + 4, t * P:t * P + qn],
                                       CD[half][:, :].rearrange("p (k q) -> p k q", q=P)[:, :, 0:qn], ACT.Identity)\
                            .then_inc(ot_evac, 1)
            SC = [setA[:, 0, :], setA[:, 1, :], setB[:, 0, :], setB[:, 1, :]]
            for h in range(4):
                act.wait_ge(s_dots, NS + 1)
                if h:
                    act.wait_ge(s_row_e, h)
                    act.wait_ge(s_relu, 2 * h)
                act.activation(relus[:, 0:PAST], SC[h][0:NS, :], ACT.Relu).then_inc(s_relu, 1)
                act.wait_ge(s_row, h + 1)
                act.activation(relus[:, PAST:PAST + 1], smn[0:NS, h:h + 1], ACT.Relu).then_inc(s_relu, 1)
            act.wait_ge(s_sc, 2 * NS + 1)
            act.activation(ps_[:, 0:PAST + 1], ss_[:, 0:PAST + 1], ACT.Exp, bias=smn[:, 0:1], scale=-1.0,
                           accum_out=smn[:, 1:2]).then_inc(s_relu, 1)
            phase_over(act, 1)

        def dve_attn(v, ch):
            v.tensor_copy(piotaf[:, :], piota[:, :]).then_inc(pidx_ready, 1)
            v.wait_ge(pidx_ready, 1)
            v.tensor_scalar(pidx[:, :], ptab[:, :], float(PS), piotaf[:, 0:1], ALU.mult, ALU.add).then_inc(pidx_ready, 1)
            phase_over(v, 0)

            def mask(u):
                t, pos = AU[u]
                qn, w = QROWS[t], WID[t]
                v.wait_ge(s_done, u + 1)
                if u >= 2:
                    v.wait_ge(exp_done, u - 1)
                v.tensor_tensor_reduce(smx[0:qn, u % 2, 0:w],
                                       SETS[u % 2][0:qn, :, :].rearrange("p a b -> p (a b)")[:, 0:w],
                                       mb[0:qn, MOFF[t]:MOFF[t] + w], -(HD ** -0.5), 3e38, ALU.add, ALU.min,
                                       nmax[0:qn, u % 2:u % 2 + 1]).then_inc(s_masked, 1)
            def result(u):
                t, pos = AU[u]
                qn = QROWS[t]
                v.wait_ge(exp_done, u + 1)
                if u >= 1:
                    v.wait_ge(o_evac, u)
                ch.run(v.reciprocal(rl[0:qn, u % 2:u % 2 + 1], lsum[0:qn, u % 2:u % 2 + 1]))
                v.wait_ge(o_done, u + 1)
                if pos == 0 and t >= 2:
                    v.wait_ge(ot_done, 2 * (t - 1))
                v.tensor_scalar(otok[0:qn, t % 2, pos * HD:(pos + 1) * HD], SETS[u % 2][0:qn, 2, 256:256 + HD],
                                rl[0:qn, u % 2:u % 2 + 1], None, ALU.mult).then_inc(o_evac, 1)

            mask(0)
            for u, (t, pos) in enumerate(AU):
                qn = QROWS[t]
                wide = u + 1 < len(AU) and WID[AU[u + 1][0]] > 1024
                if pos and wide:
                    result(u - 1)
                if u + 1 < len(AU):
                    mask(u + 1)
                dn = DCOUNT[u]
                for bank, b0, nb, kn in groups(t):
                    if bank == 1:
                        dn += 1
                        v.wait_ge(pt_done[1], dn)
                        v.tensor_copy(ptT[0:kn, u % 2, b0:b0 + nb, 0:qn],
                                      bankD[0:kn, 0:nb * P].rearrange("p (b q) -> p b q", q=P)[:, :, 0:qn])\
                            .then_inc(pt_evac[1], 1)
                if pos and not wide:
                    result(u - 1)
                if pos == NH - 1:
                    result(u)
            v.wait_ge(o_evac, len(AU))
            v.wait_ge(ot_evac, 2 * NT)
            for k in range(2):
                ch.step(v.tensor_tensor(qz[:, k, :, :], delta8[:, :, :],
                                        qis[:, k, :].unsqueeze(1).to_broadcast([P, NS, NS]), ALU.mult))
            ch.step(v.memset(qzz[:, :, :], 0.0))
            ch.settle()
            v.tensor_scalar(smn[:, :], ident[:, 0:4], 0.0, None, ALU.mult).then_inc(s_rdy, 1)
            for b in range(NS):
                for c in range(2):
                    r0 = b * NH + c * 8
                    ins = v.tensor_tensor(qzz[:, 2 * b + c, r0:r0 + 8].rearrange("p (g h) -> p g h", h=2),
                                          qT[:, 4 * c:4 * c + 4, L + b:L + b + 1].to_broadcast([P, 4, 2]),
                                          hm[:, :].unsqueeze(1).to_broadcast([P, 4, 2]), ALU.mult)
            ins.then_inc(s_rdy, 1)
            for b in range(NS):
                v.wait_ge(s_idx, b + 1)
                if b >= 2:
                    v.wait_ge(s_dots, b - 1)
                v.tensor_copy(kxT[0:HD, b % 2, :], CD[b % 2][0:HD, :])
                v.tensor_copy(kxT[HD:P, b % 2, :], CD[b % 2][0:HD, :]).then_inc(s_idx_e, 1)
            v.wait_ge(s_dots, NS + 1)
            v.wait_ge(s_rdy, 2)
            ch.settle()
            ch.run(v.tensor_scalar(kis[:, HD:68], kis[:, HD:68], (HD ** -0.5) * (4 ** -0.5), None, ALU.mult))
            for h in range(4):
                v.tensor_tensor_reduce(dg[:, :], SETS[h % 2][0:NS, 2, h * NS:(h + 1) * NS], ident[0:NS, 0:NS], 1.0, 0.0,
                                       ALU.mult, ALU.add, smn[0:NS, h:h + 1]).then_inc(s_row, 1)
                v.wait_ge(s_row, h + 1)
                v.wait_ge(s_relu, 2 * h + 2)
                if h == 0:
                    v.tensor_scalar(scs[:, 0:PAST + 1], relus[:, 0:PAST + 1], kis[:, HD:HD + 1], None, ALU.mult)\
                        .then_inc(s_row_e, 1)
                else:
                    v.scalar_tensor_tensor(scs[:, 0:PAST + 1], relus[:, 0:PAST + 1], kis[:, HD + h:HD + h + 1],
                                           scs[:, 0:PAST + 1], ALU.mult, ALU.add).then_inc(s_row_e, 1)
                v.wait_ge(s_row_e, h + 1)
            t8 = top8[0:NS, :]
            n0 = 2 * (TOPK // 8) * (NT - 2)
            with v.Fori(0, TOPK_S // 8) as i:
                v.max(t8, scs[:, 0:PAST + 1]).then_inc(topk_step, 1)
                v.wait_ge(topk_step, i * 2 + (n0 + 1))
                v.tensor_copy(held[0:NS, :], t8[:, 0:1])
                v.match_replace(scs[:, 0:PAST + 1], t8, scs[:, 0:PAST + 1], TAKEN).then_inc(topk_step, 1)
                v.wait_ge(topk_step, i * 2 + (n0 + 2))
            v.tensor_scalar(mss[:, 0:PAST + 1], scs[:, 0:PAST + 1], TAKEN * 0.5, MASKED, ALU.is_gt, ALU.mult)\
                .then_inc(s_top, 1)
            for u in range(2 * NS):
                b, c = u // 2, u % 2
                v.wait_ge(s_kT, u + 1)
                if b >= 2:
                    v.wait_ge(s_sc, 2 * (b - 2) + c + 1)
                v.tensor_copy(kgT[:, b % 2, c, :], CD[u % 2][:, :]).then_inc(s_kTe, 1)
            v.wait_ge(s_sc, 2 * NS)
            ch.step(v.tensor_scalar(ss_[:, 0:PAST], setB[:, 0, :], -(HD ** -0.5), None, ALU.mult))
            ch.run(v.tensor_scalar(ss_[:, PAST:PAST + 1], setB[:, 1, 0:1], -(HD ** -0.5), None, ALU.mult))
            v.tensor_reduce(smn[:, 0:1], ss_[:, 0:PAST + 1], AX_X, ALU.min).then_inc(s_sc, 1)
            v.wait_ge(s_relu, 9)
            ch.run(v.reciprocal(smn[:, 2:3], smn[:, 1:2]))
            v.tensor_scalar(ps_[:, 0:PAST + 1], ps_[:, 0:PAST + 1], smn[:, 2:3], None, ALU.mult).then_inc(s_exp, 1)
            v.wait_ge(s_pT, 2)
            v.tensor_copy(ptS[:, :, :], bankC[:, :].rearrange("p (g r) -> p g r", r=P)).then_inc(s_pTe, 1)
            v.tensor_copy(pnT[0:1, :], bankD[0:1, 0:P]).then_inc(s_pTe, 1)
            v.wait_ge(s_pv, 1)
            for hf in range(2):
                hs = slice(hf * HD, hf * HD + HD)
                ch.step(v.tensor_copy(qT[hs, :, L:T],
                                      setA[hs, 0, 0:P].rearrange("p (b j h) -> p j b h", b=NS, h=2)[:, :, :, hf]))
            phase_over(v, 1)

        tail_done, tail_evac, tail_saved = sem("tail_done"), sem("tail_evac"), sem("tail_saved")
        st_loaded, cs_step = sem("conv_state_loaded"), sem("sample_conv_step")
        a = Region(TREG, SCR - TREG)
        tailtok = a.take("tailtok", [24, CONVD])
        a = Region(BASE, 2 * XB)
        sconv = a.take("sconv", [NS * 3, CONVD])
        csT = a.take("csT", [P, CONVD // P, NS * 3])
        xcs = a.take("xcs", [P, CONVD // P, NS])
        ctmp = a.take("ctmp", [P, CONVD // P, NS])
        NB = CONVD // P

        def sp_convtail(sp):
            for j in range(2):
                sp.wait_ge(gemm_done[j], 3 * ORD_AO)
            sp.dma_start(sconv[:, :], A["state_conv"][0].rearrange("b j c -> (b j) c")).then_inc(st_loaded, 16)
            for b in range(NS):
                store(sp, O["conv_sample"][0, b, 0:2], A["state_conv"][0, b, 1:3])

        def pe_convtail(pe):
            pe.wait_ge(conv_done, 24)
            for j in range(2):
                pe.wait_ge(gemm_evac[j], 3 * ORD_AO)
            for b in range(NB):
                mm = pe.transpose(SETS[b // 12][0:24, b % 12 // 4, b % 4 * P:(b % 4 + 1) * P], rtail[:, b, :], ident[:, :])
            mm.then_inc(tail_done, 1)
            pe.wait_ge(st_loaded, 16)
            for b in range(NB):
                mm = pe.transpose(CD[b // 12][:, b % 12 * 24:(b % 12 + 1) * 24], sconv[:, b * P:(b + 1) * P],
                                  ident[0:24, 0:24])
            mm.then_inc(tail_done, 1)

        def act_convtail(act):
            act.wait_ge(tail_done, 1)
            act.wait_ge(conv_silu, 24)
            for j in range(2):
                act.wait_ge(spill_out[j], 16 * 16)
                act.wait_ge(conv_out[j], 16 * 12)
            for s in range(2):
                act.activation(tailtok[:, s * 1536:(s + 1) * 1536], SETS[s][0:24, :, :].rearrange("p a b -> p (a b)"),
                               ACT.Identity).then_inc(tail_evac, 1)
            act.wait_ge(tail_evac, 2)
            act.dma_start(O["conv_prompt"][0, 0], tailtok[LAST - 3:LAST, :]).then_inc(tail_saved, 16)
            act.dma_start(O["conv_sample"][0, :, 2], tailtok[LAST:24, :]).then_inc(tail_saved, 16)
            act.wait_ge(cs_step, 10)
            act.activation(xcs[:, :, :], xcs[:, :, :], ACT.Silu).then_inc(tail_evac, 1)
            act.wait_ge(tail_evac, 3)
            act.dma_start(xcD.rearrange("(b p) t -> p b t", p=P)[:, :, L:T], xcs[:, :, :]).then_inc(tail_saved, 16)
            act.wait_ge(tail_saved, 48)

        def dve_convtail(v):
            v.wait_ge(tail_done, 2)
            for s in range(2):
                v.tensor_copy(csT[:, 12 * s:12 * s + 12, :], CD[s][:, 0:288].rearrange("p (b c) -> p b c", c=24))\
                    .then_inc(cs_step, 1)
            v.wait_ge(cs_step, 2)
            taps = [csT[:, :, j:24:3] for j in range(3)]
            taps.append(rtail[:, :, LAST:24])
            n = 2
            for j, x_ in enumerate(taps):
                dst = xcs if j == 0 else ctmp
                v.tensor_tensor(dst[:, :, :], x_, cw[:, :, j:j + 1].to_broadcast([P, NB, NS]), ALU.mult).then_inc(cs_step, 1)
                n += 1
                v.wait_ge(cs_step, n)
                other = cb[:, :].unsqueeze(2).to_broadcast([P, NB, NS]) if j == 0 else ctmp[:, :, :]
                v.tensor_tensor(xcs[:, :, :], xcs[:, :, :], other, ALU.add).then_inc(cs_step, 1)
                n += 1
                v.wait_ge(cs_step, n)

        NCH = 1 + SEQ // P
        GW = DI // SG
        HG = SH // SG
        GB = GW // P
        NXB = DI // P
        DTOFF = AR + (2 * T + NT * 256) * 4
        a = Region(BASE, 2 * XB)
        xc = a.take("xc", [P, 2, NB, P])
        abc = a.take("abc", [P, 2, SH, P])
        a = Region(AR, DTOFF - AR)
        y2 = a.take("y2", [P, 2, NXB, P])
        a = Region(mboff, AEND - mboff)
        hT = a.take("hT", [P, DI])
        zc = a.take("zc", [P, 2, NXB, P])
        es = at("es", [P, 2, HG, P], F32, WHI)
        ce = at("ce", [P, 2, HG, P], F32, WHI + 2 * HG * P * 4)
        xdt = a.take("xdt", [P, 2, GW])
        xw = a.take("xw", [P, 2, GW])
        btok = a.take("btok", [P, 2, P])
        cbm = a.take("cbm", [P, 2, P])
        ysq = a.take("ysq", [P, 2, GB, P])
        ss4 = a.take("ss4", [P, 2, SG, P])
        ttok = a.take("ttok", [P, NCH, 2 * SH])
        tc = a.take("tc", [P, 2, 2 * SH])
        ed = a.take("ed", [P, 2, SH])
        cd = a.take("cd", [P, 2, SH])
        acsT = a.take("acsT", [SH, T])
        dn = at("dn", [SH, T], F32, BASE)
        dt_t = at("dt_t", [SH, T], F32, BASE + T * 4)
        dl = at("dl", [SH, T], F32, BASE + 2 * T * 4)
        de = at("de", [SH, T], F32, BASE + 3 * T * 4)

        dt_step, dt_exp, acs_ready, acs_stored = (sem(n) for n in ("dt_step", "dt_exp", "acs_ready", "acs_stored"))
        tt_done, tt_evac = sem("token_dt_T"), sem("token_dt_evac")
        chunk_loaded = [sem("chunk_loaded0"), sem("chunk_loaded1")]
        (front_done, seg_ready, seg_exp, ce_exp, ce_ready, xdt_ready, m_ready, xw_ready, y_done, st_done,
         hc_done, h_added, y1_step, y2_ready, ysq_ready, ssq_done, ssq_copied, small_ready, small_exp, root_done,
         rstd_ready, norm_ready) = (sem("ssd_" + n) for n in (
             "front", "seg", "seg_exp", "ce_exp", "ce", "xdt", "m", "xw", "y", "state", "h_decayed", "h_added",
             "y1", "y2", "ysq", "ssq", "ssq_copied", "small", "small_exp", "root", "rstd", "normed"))
        s_stored = [sem("s_stored0"), sem("s_stored1")]
        fin_done, fin_evac = sem("state_T"), sem("state_T_evac")

        def tok0(c):
            if isinstance(c, int):
                return (0, META) if c == 0 else (META + (c - 1) * P, P)
            return c * P + (META - P), P

        def over_chunks(eng, step):
            step(0, 0, 0, 1)
            step(1, 1, 0, 2)
            with eng.Fori(0, (NCH - 3) // 2) as i:
                step(i * 2 + 2, 0, i + 1, i * 2 + 3)
                step(i * 2 + 3, 1, i + 1, i * 2 + 4)
            step(NCH - 1, 0, NCH // 2, None)

        def wait_u(eng, s, c, g, back):
            if isinstance(c, int) and 4 * c + g + 1 - back <= 0:
                return
            eng.wait_ge(s, c * 4 + (g + 1 - back))

        def following(c, g, nxt):
            return (c, g + 1) if g < SG - 1 else (None if nxt is None else (nxt, 0))

        def before(c, g, back):
            if g >= back:
                return c, g - back
            if isinstance(c, int) and c == 0:
                return None
            return c - 1, g - back + SG

        def width(c):
            return META if isinstance(c, int) and c == 0 else P

        def slot_of(c, g, slot):
            return slot if g < SG - 1 else 1 - slot

        def sp_ssd(sp):
            def load(c, slot):
                o, w = tok0(c)
                ts = bass.ds(o, w)
                sp.dma_start(xc[:, slot, :, 0:w], xcD.rearrange("(b p) t -> p b t", p=P)[:, :, ts])\
                    .then_inc(chunk_loaded[slot], 16)
                sp.dma_start(zc[:, slot, :, 0:w], zD.rearrange("(b p) t -> p b t", p=P)[:, :, ts])\
                    .then_inc(chunk_loaded[slot], 16)
                sp.dma_start(abc[:, slot, :, 0:w], acsD[:, ts].partition_broadcast(P)).then_inc(chunk_loaded[slot], 16)

            def step(c, slot, used, nxt):
                o, w = tok0(c)
                sp.wait_ge(norm_ready, c * NXB + NXB)
                sp.dma_start(sD.rearrange("(b p) t -> p b t", p=P)[:, :, bass.ds(o, w)], y2[:, slot, :, 0:w])\
                    .then_inc(s_stored[slot], 16)
            sp.wait_ge(acs_stored, 48)
            sp.wait_ge(tt_evac, 2)
            load(0, 0)
            load(1, 1)
            sp.wait_ge(y2_ready, 4)
            load(2, 0)
            step(0, 0, 0, 1)
            with sp.Fori(0, (NCH - 3) // 2) as i:
                sp.wait_ge(y2_ready, i * 8 + 8)
                load(i * 2 + 3, 1)
                step(i * 2 + 1, 1, 0, None)
                sp.wait_ge(y2_ready, i * 8 + 12)
                load(i * 2 + 4, 0)
                step(i * 2 + 2, 0, 0, None)
            step(NCH - 2, 1, 0, None)
            step(NCH - 1, 0, 0, None)
            for m in range(NXB // 4):
                sp.wait_ge(fin_evac, m + 1)
                sp.dma_start(O["ssm_prompt"][0, 0].rearrange("e p n -> (e p) n")[m * 512:(m + 1) * 512, :]
                             .rearrange("(b q) n -> q b n", q=P), fin_st[:, m, :, :]).then_inc(s_stored[0], 16)
            sp.wait_ge(s_stored[0], 16 * (NCH // 2 + 1 + NXB // 4))
            sp.wait_ge(s_stored[1], 16 * (NCH // 2))
            phase_over(sp, 2)

        fin_st = at("fin_st", [P, NXB // 4, 4, P], F32, BASE)

        def pe_ssd(pe):
            pe.wait_ge(acs_ready, 1)
            for c in range(NCH):
                o, w = tok0(c)
                for k, src in enumerate((dtT, acsT)):
                    mm = pe.transpose(CD[c // 5][0:w, c % 5 * 64 + k * SH:c % 5 * 64 + (k + 1) * SH], src[:, o:o + w],
                                      ident[0:SH, 0:SH])
                if c in (4, NCH - 1):
                    mm.then_inc(tt_done, 1)
            pe.wait_ge(tt_evac, 2)

            def front(c, g, slot, used):
                w, s = width(c), g % 2
                if g == 0:
                    pe.wait_ge(chunk_loaded[slot], used * 48 + 48)
                wait_u(pe, xdt_ready, c, g, 1)
                pe.matmul(bankC[0:w, 0:w], xc[:, slot, NXB + g, 0:w], xc[:, slot, NXB + SG + g, 0:w], start=True, stop=True)
                pe.transpose(bankC[0:w, P:2 * P], xc[:, slot, NXB + g, 0:w], ident[:, :])
                for m in range(GB):
                    mm = pe.transpose(SETS[s][0:w, 2, m * P:(m + 1) * P], xc[:, slot, GB * g + m, 0:w], ident[:, :])
                mm.then_inc(front_done, 1)

            def ssq(c, g):
                w, s = width(c), g % 2
                wait_u(pe, ysq_ready, c, g, 0)
                wait_u(pe, ssq_copied, c, g, 1)
                for m in range(GB):
                    mm = pe.matmul(bankD[:, 0:w], ones[:, :], ysq[:, s, m, 0:w], start=m == 0, stop=m == GB - 1)
                mm.then_inc(ssq_done, 1)

            def step(c, slot, used, nxt):
                w = width(c)
                for g in range(SG):
                    s = g % 2
                    n = following(c, g, nxt)
                    if n is not None:
                        front(n[0], n[1], slot_of(c, g, slot), used if g < SG - 1 or slot == 0 else used + 1)
                    two = before(c, g, 2)
                    if two is not None:
                        ssq(*two)
                    wait_u(pe, m_ready, c, g, 0)
                    wait_u(pe, ce_ready, c, g, 0)
                    wait_u(pe, h_added, c, g, SG)
                    wait_u(pe, y2_ready, c, g, 2)
                    for e in range(HG):
                        out = SETS[s][(e % 2) * HD:(e % 2 + 1) * HD, 0, (e // 2) * P:(e // 2) * P + w]
                        pe.matmul(out, xdt[0:w, s, e * HD:(e + 1) * HD], es[0:w, s, e, 0:w], start=True, stop=False)
                        mm = pe.matmul(out, hT[:, (HG * g + e) * HD:(HG * g + e + 1) * HD], ce[:, s, e, 0:w],
                                       start=False, stop=True)
                    mm.then_inc(y_done, 1)
                    wait_u(pe, xw_ready, c, g, 0)
                    wait_u(pe, h_added, c, g, 2)
                    pe.matmul(SETS[s][:, 1, :], btok[0:w, s, :], xw[0:w, s, :], start=True, stop=True).then_inc(st_done, 1)
            pe.wait_ge(hT_zero, 1)
            front(0, 0, 0, 0)
            over_chunks(pe, step)
            ssq(NCH - 1, SG - 2)
            ssq(NCH - 1, SG - 1)
            pe.wait_ge(h_added, 4 * NCH)
            for m in range(NXB // 4):
                if m >= 2:
                    pe.wait_ge(fin_evac, m - 1)
                for k in range(4):
                    mm = pe.transpose(SETS[m % 2][:, 0, k * P:(k + 1) * P], hT[:, (4 * m + k) * P:(4 * m + k + 1) * P],
                                      ident[:, :])
                mm.then_inc(fin_done, 1)
            phase_over(pe, 2)

        hT_zero = sem("state_zeroed")

        def act_ssd(act):
            act.wait_ge(dt_step, 2)
            act.activation(dt_t[:, :], dn[:, :], ACT.Exp).then_inc(dt_exp, 1)
            act.activation(nega[:, :], nega[:, :], ACT.Exp).then_inc(dt_exp, 1)
            act.wait_ge(dt_step, 3)
            act.activation(dl[:, :], dl[:, :], ACT.Ln).then_inc(dt_exp, 1)

            act.wait_ge(acs_ready, 1)
            act.dma_start(acsD[:, :], acsT[:, :]).then_inc(acs_stored, 16)
            act.dma_start(smD[0], dtT[:, L:T]).then_inc(acs_stored, 16)
            act.dma_start(smD[1], acsT[:, L:T]).then_inc(acs_stored, 16)

            def exps(c, g, slot, used):
                w, s = width(c), g % 2
                hs = slice(HG * g, HG * g + HG)
                if g == 0:
                    act.wait_ge(chunk_loaded[slot], used * 48 + 48)
                    act.activation(cd[:, slot, :], abc[:, slot, :, w - 1], ACT.Exp)
                    act.wait_ge(small_ready, c * 2 + 2)
                    act.activation(ed[0:w, slot, :], ed[0:w, slot, :], ACT.Exp).then_inc(small_exp, 1)
                wait_u(act, y_done, c, g, 2)
                act.activation(ce[:, s, :, 0:w], abc[:, slot, hs, 0:w], ACT.Exp).then_inc(ce_exp, 1)
                wait_u(act, seg_ready, c, g, 0)
                act.activation(es[0:w, s, :, 0:w], es[0:w, s, :, 0:w], ACT.Exp).then_inc(seg_exp, 1)

            def square(c, g, slot):
                w, s = width(c), g % 2
                wait_u(act, y2_ready, c, g, 0)
                wait_u(act, ssq_done, c, g, 2)
                act.activation(ysq[:, s, :, 0:w], y2[:, slot, GB * g:GB * g + GB, 0:w], ACT.Square)\
                    .then_inc(ysq_ready, 1)

            def ssq_copy(c, g, slot):
                w = width(c)
                wait_u(act, ssq_done, c, g, 0)
                if g == 0 and not (isinstance(c, int) and c < 2):
                    act.wait_ge(norm_ready, c * NXB - NXB)
                act.activation(ss4[:, slot, g, 0:w], bankD[:, 0:w], ACT.Identity).then_inc(ssq_copied, 1)
                if g == SG - 1:
                    act.wait_ge(ssq_copied, c * 4 + 4)
                    act.activation(ss4[:, slot, :, 0:w], ss4[:, slot, :, 0:w], ACT.Sqrt, bias=eps[:, 0:1],
                                   scale=1.0 / GW).then_inc(root_done, 1)

            def step(c, slot, used, nxt):
                w = width(c)
                for g in range(SG):
                    s = g % 2
                    n = following(c, g, nxt)
                    if n is not None:
                        exps(n[0], n[1], slot_of(c, g, slot), used if g < SG - 1 or slot == 0 else used + 1)
                    two, one = before(c, g, 2), before(c, g, 1)
                    if two is not None:
                        ssq_copy(*two, slot if g >= 2 else 1 - slot)
                    if one is not None:
                        square(*one, slot if g >= 1 else 1 - slot)
            exps(0, 0, 0, 0)
            over_chunks(act, step)
            ssq_copy(NCH - 1, SG - 2, 0)
            square(NCH - 1, SG - 1, 0)
            ssq_copy(NCH - 1, SG - 1, 0)
            act.wait_ge(acs_stored, 48)
            phase_over(act, 2)

        def pool_ssd(pool, ch):
            pool.memset(hT[:, :], 0.0).then_inc(hT_zero, 1)
            pool.wait_ge(hT_zero, 1)

            def scaled(c, g, slot):
                w, s = width(c), g % 2
                hs = slice(HG * g, HG * g + HG)
                wait_u(pool, ce_exp, c, g, 0)
                pool.tensor_tensor(ce[:, s, :, 0:w], ce[:, s, :, 0:w],
                                   xc[:, slot, NXB + SG + g, 0:w].unsqueeze(1).to_broadcast([P, HG, w]), ALU.mult)\
                    .then_inc(ce_ready, 1)
                wait_u(pool, xdt_ready, c, g, 0)
                if g == 0:
                    pool.wait_ge(small_exp, c + 1)
                wait_u(pool, st_done, c, g, 2)
                pool.tensor_tensor(xw[0:w, s, :].rearrange("p (e q) -> p e q", e=HG),
                                   xdt[0:w, s, :].rearrange("p (e q) -> p e q", e=HG),
                                   ed[0:w, slot, hs].unsqueeze(2).to_broadcast([w, HG, HD]), ALU.mult)\
                    .then_inc(xw_ready, 1)

            def step(c, slot, used, nxt):
                for g in range(SG):
                    n = following(c, g, nxt)
                    if n is not None:
                        scaled(n[0], n[1], slot_of(c, g, slot))
                    hh_ = hT[:, g * GW:(g + 1) * GW].rearrange("p (e q) -> p e q", e=HG)
                    wait_u(pool, y_done, c, g, 0)
                    pool.tensor_tensor(hh_, hh_, cd[:, slot, HG * g:HG * g + HG].unsqueeze(2).to_broadcast([P, HG, HD]),
                                       ALU.mult).then_inc(hc_done, 1)
            scaled(0, 0, 0)
            over_chunks(pool, step)
            phase_over(pool, 2)

        def dve_ssd(v, ch):
            v.tensor_scalar(dtT[:, :], dtT[:, :], dtb[:, 0:1], None, ALU.add).then_inc(dt_step, 1)
            v.wait_ge(dt_step, 1)
            v.scalar_tensor_tensor(dn[:, :], dtT[:, :], -1.0, dtT[:, :], ALU.mult, ALU.min).then_inc(dt_step, 1)
            v.wait_ge(dt_exp, 1)
            v.tensor_scalar(dl[:, :], dt_t[:, :], 1.0, None, ALU.add).then_inc(dt_step, 1)
            v.wait_ge(dt_step, 3)
            ch.run(v.tensor_scalar(de[:, :], dt_t[:, :], 1.0, -1.0, ALU.add, ALU.add))
            ch.run(v.tensor_scalar(dn[:, :], de[:, :], 0.0, None, ALU.is_equal))
            ch.run(v.tensor_tensor(de[:, :], de[:, :], dn[:, :], ALU.add))
            v.wait_ge(dt_exp, 3)
            ch.run(v.tensor_tensor(dl[:, :], dl[:, :], dn[:, :], ALU.add))
            ch.run(v.reciprocal(de[:, :], de[:, :]))
            ch.run(v.tensor_tensor(dl[:, :], dl[:, :], de[:, :], ALU.mult))
            ch.run(v.tensor_tensor(dl[:, :], dl[:, :], dt_t[:, :], ALU.mult))
            ch.run(v.scalar_tensor_tensor(dtT[:, :], dtT[:, :], 0.0, dl[:, :], ALU.max, ALU.add))
            ch.run(v.tensor_scalar(nega[:, :], nega[:, :], -1.0, None, ALU.mult))
            ch.run(v.tensor_scalar(dn[:, :], dtT[:, :], nega[:, 0:1], None, ALU.mult))
            ch.run(v.memset(de[:, :], 1.0))
            for c in range(NCH):
                o, w = tok0(c)
                ch.step(v.tensor_tensor_scan(acsT[:, o:o + w], de[:, o:o + w], dn[:, o:o + w], 0.0, ALU.mult, ALU.add))
            v.tensor_copy(acsT[:, L:T], dn[:, L:T]).then_inc(acs_ready, 1)
            v.wait_ge(tt_done, 2)
            v.tensor_copy(ttok[:, 0:5, :], bankC[:, 0:320].rearrange("p (c f) -> p c f", f=64)).then_inc(tt_evac, 1)
            v.tensor_copy(ttok[:, 5:NCH, :], bankD[:, 0:(NCH - 5) * 64].rearrange("p (c f) -> p c f", f=64))\
                .then_inc(tt_evac, 1)
            v.wait_ge(tt_evac, 2)

            def seg(c, g, slot, used):
                w, s = width(c), g % 2
                if g == 0:
                    v.wait_ge(chunk_loaded[slot], used * 48 + 48)
                    v.tensor_copy(tc[0:w, slot:slot + 1, :], ttok[0:w, bass.ds(c, 1), :]).then_inc(small_ready, 1)
                    v.wait_ge(small_ready, c * 2 + 1)
                    v.tensor_tensor(ed[0:w, slot, :], abc[0:w, slot, :, w - 1], tc[0:w, slot, SH:2 * SH],
                                    ALU.subtract).then_inc(small_ready, 1)
                wait_u(v, y_done, c, g, 2)
                for e in range(HG):
                    h = HG * g + e
                    ins = v.tensor_scalar(es[0:w, s, e, 0:w], abc[0:w, slot, h, 0:w], tc[0:w, slot, SH + h:SH + h + 1],
                                          0.0, ALU.subtract, ALU.min)
                ins.then_inc(seg_ready, 1)
                wait_u(v, front_done, c, g, 0)
                wait_u(v, m_ready, c, g, 2)
                wait_u(v, xw_ready, c, g, 2)
                wait_u(v, st_done, c, g, 2)
                v.tensor_copy(btok[0:w, s, :], bankC[0:w, P:2 * P])
                v.tensor_tensor(cbm[0:w, s, 0:w], bankC[0:w, 0:w], tri[0:w, 0:w], ALU.mult)
                v.tensor_tensor(xdt[0:w, s, :].rearrange("p (e q) -> p e q", e=HG),
                                SETS[s][0:w, 2, :].rearrange("p (e q) -> p e q", e=HG),
                                tc[0:w, slot, HG * g:HG * g + HG].unsqueeze(2).to_broadcast([w, HG, HD]), ALU.mult)\
                    .then_inc(xdt_ready, 1)

            def weights(c, g, slot):
                w, s = width(c), g % 2
                wait_u(v, seg_exp, c, g, 0)
                wait_u(v, xdt_ready, c, g, 0)
                v.tensor_tensor(es[0:w, s, :, 0:w], es[0:w, s, :, 0:w],
                                cbm[0:w, s, 0:w].unsqueeze(1).to_broadcast([w, HG, w]), ALU.mult).then_inc(m_ready, 1)

            def gate(c, g, slot, used):
                w, s = width(c), g % 2
                wait_u(v, y_done, c, g, 0)
                if g == 0 and not (isinstance(c, int) and c < 2):
                    v.wait_ge(s_stored[slot], used * 16)
                for m in range(GB):
                    b = GB * g + m
                    ins = v.scalar_tensor_tensor(y2[:, slot, b, 0:w], xc[:, slot, b, 0:w], dsk[:, b:b + 1],
                                                 SETS[s][:, 0, m * P:m * P + w], ALU.mult, ALU.add)
                ins.then_inc(y1_step, 1)
                wait_u(v, y1_step, c, g, 0)
                bs = slice(GB * g, GB * g + GB)
                v.tensor_tensor(y2[:, slot, bs, 0:w], y2[:, slot, bs, 0:w], zc[:, slot, bs, 0:w], ALU.mult)\
                    .then_inc(y2_ready, 1)

            def state(c, g):
                wait_u(v, st_done, c, g, 0)
                wait_u(v, hc_done, c, g, 0)
                hs = slice(g * GW, (g + 1) * GW)
                v.tensor_tensor(hT[:, hs], hT[:, hs], SETS[g % 2][:, 1, :], ALU.add).then_inc(h_added, 1)

            def norm(c, slot):
                w = width(c)
                v.wait_ge(root_done, c + 1)
                v.wait_ge(y2_ready, c * 4 + 4)
                v.reciprocal(ss4[:, slot, :, 0:w], ss4[:, slot, :, 0:w]).then_inc(rstd_ready, 1)
                v.wait_ge(rstd_ready, c + 1)
                for b in range(NXB):
                    v.scalar_tensor_tensor(y2[:, slot, b, 0:w], y2[:, slot, b, 0:w], gssd[:, b:b + 1],
                                           ss4[:, slot, b // GB, 0:w], ALU.mult, ALU.mult).then_inc(norm_ready, 1)

            def step(c, slot, used, nxt):
                for g in range(SG):
                    n = following(c, g, nxt)
                    ns = slot_of(c, g, slot)
                    if n is not None:
                        seg(n[0], n[1], ns, used if g < SG - 1 or slot == 0 else used + 1)
                    one = before(c, g, 1)
                    if one is not None:
                        gate(*one, slot if g else 1 - slot, used if g or slot == 1 else used - 1)
                        state(*one)
                    if n is not None:
                        weights(n[0], n[1], ns)
                    if g == 2 and not (isinstance(c, int) and c == 0):
                        norm(c - 1, 1 - slot)
            v.wait_ge(hT_zero, 1)
            seg(0, 0, 0, 0)
            weights(0, 0, 0)
            over_chunks(v, step)
            gate(NCH - 1, SG - 1, 0, NCH // 2)
            state(NCH - 1, SG - 1)
            norm(NCH - 1, 0)
            v.wait_ge(norm_ready, NXB * NCH)
            for m in range(NXB // 4):
                v.wait_ge(fin_done, m + 1)
                v.tensor_copy(fin_st[:, m, :, :], SETS[m % 2][:, 0, :].rearrange("p (b n) -> p b n", n=P))\
                    .then_inc(fin_evac, 1)
            phase_over(v, 2)

        mixed = at("mixed", [P, KD, T], F32, R1)
        a = Region(AR, AEND - AR)
        sraw = a.take("sraw", [P, KD, T])
        acc = a.take("acc", [P, KD, T])
        gates = a.take("gates", [P, 3, 2, 352])
        a = Region(AR, AEND - AR)
        h0 = a.take("h0", [P, 2, NXB, DSTATE])
        hn = a.take("hn", [P, 2, NXB, DSTATE])
        bx = a.take("bx", [P, 2, NXB, DSTATE])
        bcb = a.take("bcb", [P, 2, 2 * SG * DSTATE])
        xss = a.take("xss", [P, NB, NS])
        zss = a.take("zss", [P, NXB, NS])
        smb = a.take("smb", [P, 2, NXB, NS])
        ys = a.take("ys", [P, NXB, NS])
        ysr = a.take("ysr", [P, NXB, NS])
        rss = a.take("rss", [P, SG, NS])
        bct = at("bct", [NS, 2 * SG * DSTATE], F32, a.cur)
        xre = at("xre", [P, KD, T], F32, AR)
        yout = at("yout", [P, 2, D], F32, AR)

        smp_loaded, bct_done, bct_evac, bc_stored = (
            sem("ssds_" + n) for n in ("loaded", "bc_T", "bc_evac", "bc_stored"))
        bc_loaded = [sem("bc_loaded0"), sem("bc_loaded1")]
        h0_loaded = [sem("h0_loaded0"), sem("h0_loaded1")]
        hn_stored = [sem("hn_stored0"), sem("hn_stored1")]
        h0_decayed, bx_ready, hn_ready, ys_done, ys_ss = (
            sem("ssds_" + n) for n in ("decayed", "bx", "hn", "y", "ss"))
        smp_dve = sem("ssds_vector_part")
        smp_act = sem("ssds_scalar_part")
        part_hi = sem("part_hi")
        part_ready = sem("part_ready")
        sraw_loaded = sem("sraw_loaded")
        gates_loaded = [sem(f"gates_loaded{c}") for c in range(3)]
        mix_ready = sem("mix_ready")
        y_T, y_evac = sem("y_T"), [sem("y_evac_dve"), sem("y_evac_act")]
        y_stored = [sem("y_stored0"), sem("y_stored1")]
        PART_ORD = [ORD_AO, ORD_SO, ORD_SO + 4, ORD_WO]

        def sp_tail(sp):
            ao = A["w_attn_out"][0].rearrange("(c h g p) n -> c h p g n", c=2, h=2, g=4)

            def load_ao(m):
                sp.wait_ge(w_split, TILE_AO + m - 1)
                for c in range(2):
                    for h in range(2):
                        sp.dma_start(wraw[h * HD:(h + 1) * HD, m % 2, c * 512:(c + 1) * 512]
                                     .rearrange("p (g n) -> p g n", g=4), ao[c, h][:, :, m * P:(m + 1) * P])\
                            .then_inc(raw_loaded[m % 2], 16)

            def load_bc(b):
                sp.dma_start(bcb[:, b % 2, :], bcD[b].partition_broadcast(P)).then_inc(bc_loaded[b % 2], 16)

            def load_h0(b):
                if b >= 2:
                    sp.wait_ge(ys_done, 2 * (b - 1))
                sp.dma_start(h0[:, b % 2, :, :], A["state_ssm"][0, b].rearrange("e p n -> (e p) n")
                             .rearrange("(k q) n -> q k n", q=P)).then_inc(h0_loaded[b % 2], 16)
            load_ao(0)
            load_ao(1)
            load_h0(0)
            load_h0(1)
            for k in range(2):
                for h in range(2):
                    sp.dma_start(smb[h * HD:(h + 1) * HD, k, :, :],
                                 smD[k].rearrange("(m h) b -> h m b", h=2)[h].partition_broadcast(HD))\
                        .then_inc(smp_loaded, 16)
            sp.dma_start(xss[:, :, :], xcD.rearrange("(b p) t -> p b t", p=P)[:, :, L:T]).then_inc(smp_loaded, 16)
            sp.dma_start(zss[:, :, :], zD.rearrange("(b p) t -> p b t", p=P)[:, :, L:T]).then_inc(smp_loaded, 16)
            sp.wait_ge(bct_evac, 2)
            sp.dma_start(bcD[:, :], bct[:, :]).then_inc(bc_stored, 16)
            sp.wait_ge(bc_stored, 16)
            load_bc(0)
            load_bc(1)
            for b in range(NS):
                if b + 2 < KD:
                    load_ao(b + 2)
                sp.wait_ge(hn_ready, b + 1)
                sp.dma_start(O["ssm_sample"][0, b].rearrange("e p n -> (e p) n").rearrange("(k q) n -> q k n", q=P),
                             hn[:, b % 2, :, :]).then_inc(hn_stored[b % 2], 16)
                if b + 2 < NS:
                    load_h0(b + 2)
                    load_bc(b + 2)
            so = A["w_ssd_out"][0]
            for j in range(2):
                load_tile(sp, TILE_SO + j, 0, j, col_tile(so[0:D, :], j * P))
            sp.wait_ge(smp_dve, 3)
            sp.dma_start(sD.rearrange("(b p) t -> p b t", p=P)[:, :, L:T], ys[:, :, :]).then_inc(bc_stored, 16)
            sp.wait_ge(bc_stored, 32)
            for i in range(2):
                sp.wait_ge(hn_stored[i], 16 * NS // 2)
            sp.dma_start(sraw[:, :, :], sD[0:D, :].rearrange("(k p) t -> p k t", p=P)).then_inc(sraw_loaded, 16)
            with sp.Fori(0, 3) as i:
                for j in range(2):
                    load_tile(sp, i * 2 + (TILE_SO + 2 + j), 0, j, col_tile(so[0:D, :], i * 256 + (256 + j * P)))
            sp.wait_ge(part_ready, 6)
            sp.dma_start(sraw[:, :, :], sD[D:2 * D, :].rearrange("(k p) t -> p k t", p=P)).then_inc(sraw_loaded, 16)

            def load_gates(m):
                for c, (o, w) in enumerate(CH):
                    if m:
                        sp.wait_ge(mix_ready, 3 * (m - 1) + c + 1)
                    for k, g_ in enumerate((gaD, gsD)):
                        sp.dma_start(gates[:, c, k, 0:w], g_[m * P:(m + 1) * P, o:o + w]).then_inc(gates_loaded[c], 16)
            load_gates(0)
            for m in range(KD):
                load_tile(sp, TILE_SO + KD + m, 0, m % 2, col_tile(so[D:2 * D, :], m * P))
                if m == 1:
                    sp.wait_ge(part_ready, 9)
                    sp.dma_start(xre[:, :, :], xD.rearrange("(k p) t -> p k t", p=P)).then_inc(sraw_loaded, 16)
                if m >= 2:
                    load_gates(m - 1)
            load_gates(KD - 1)
            with sp.Fori(0, 4) as i:
                for j in range(2):
                    load_tile(sp, i * 2 + (TILE_WO + j), 0, j, col_tile(A["w_o"][0], i * 256 + j * P))
            sp_ffn(sp, 1)
            for t in range(NT):
                s = t % 2
                sp.wait_ge(y_evac[0], t + 1)
                sp.wait_ge(y_evac[1], t + 1)
                r0 = max(0, t * P - META)
                if t < NT - 1:
                    sp.dma_start(O["y_prompt"][0, r0:(t + 1) * P - META, :], yout[META if t == 0 else 0:P, s, :])\
                        .then_inc(y_stored[s], 16)
                else:
                    sp.dma_start(O["y_prompt"][0, r0:SEQ, :], yout[0:LAST, s, :]).then_inc(y_stored[s], 16)
                    sp.dma_start(O["y_sample"].rearrange("b s d -> (b s) d"), yout[LAST:LAST + NS, s, :])\
                        .then_inc(y_stored[s], 16)
            sp.wait_ge(y_stored[0], 16 * (NT // 2 + 2))
            sp.wait_ge(y_stored[1], 16 * (NT // 2))

        def pool_tail(pool, ch):
            for i in range(KD):
                split_tile(pool, TILE_AO + i, raw_count(TILE_AO + i) + 3, i % 2, (gemm_done[i % 2], 3 * (ORD_AO + i // 2)))
                b, s = i, i % 2
                if i == 0:
                    pool.wait_ge(smp_dve, 1)
                pool.wait_ge(bc_loaded[s], 16 * (b // 2) + 16)
                if i >= 2:
                    pool.wait_ge(hn_ready, b - 1)
                pool.tensor_tensor(bx[:, s, :, :].rearrange("p (g k) n -> p g k n", g=SG),
                                   bcb[:, s, 0:SG * DSTATE].rearrange("p (g n) -> p g n", g=SG).unsqueeze(2)
                                   .to_broadcast([P, SG, GB, DSTATE]),
                                   smb[:, 0, :, b].rearrange("p (g k) -> p g k", g=SG).unsqueeze(3)
                                   .to_broadcast([P, SG, GB, DSTATE]), ALU.mult).then_inc(bx_ready, 1)
            pool_rest(pool, TILE_SO, ORD_SO, 12)
            pool_ffn(pool, 1)

        def pe_tail(pe):
            pe.wait_ge(smp_loaded, 96)
            for half in range(2):
                for k in range(4):
                    mm = pe.transpose(CD[half][0:NS, k * P:(k + 1) * P], xss[:, NXB + 4 * half + k, :], ident[:, :])
                mm.then_inc(bct_done, 1)
            for m in range(KD):
                gemm_tile(pe, TILE_AO + m, ORD_AO + m // 2, m % 2, ready=(part_ready, 0) if m == 0 else None)
            pe.wait_ge(smp_dve, 2)
            pe.matmul(bankC[:, 0:NXB * NS], ones[:, :], ysr[:, :, :].rearrange("p k b -> p (k b)"),
                      start=True, stop=True).then_inc(ys_ss, 1)
            for s in (1, 2, 3):
                n, q = (TILE_AO + 8 * s, PART_ORD[s])
                for m in range(2):
                    gemm_tile(pe, n + m, q, m, ready=(part_ready, 3 * s) if m == 0 else None)
                with pe.Fori(0, 3) as i:
                    for j in range(2):
                        gemm_tile(pe, i * 2 + (n + 2 + j), i + (q + 1), j)
            pe_norm(pe, 2)
            pe_ffn(pe, 1)
            pe.wait_ge(down_evac, 48 * NI)
            for t in range(NT):
                o, _, w = trow(t)
                if t >= 2:
                    pe.wait_ge(y_evac[0], t - 1)
                    pe.wait_ge(y_evac[1], t - 1)
                for k in range(KD):
                    mm = pe.transpose(SETS[t % 2][0:w, k // 4, k % 4 * P:(k % 4 + 1) * P], X[:, k, o:o + w], ident[:, :])
                mm.then_inc(y_T, 1)

        def act_part(act, s, src, ready):
            for c, (o, w) in enumerate(CH):
                act.wait_ge(ready[0], ready[1] + ready[2] * c)
                if s:
                    act.wait_ge(gemm_done[1], 3 * (PART_ORD[s] - 1) + c + 1)
                act.activation(hhi[:, :, o:o + w], src[:, :, o:o + w], ACT.Identity).then_inc(part_hi, 1)

        def dve_part(v, s, src):
            for c, (o, w) in enumerate(CH):
                v.wait_ge(part_hi, 3 * s + c + 1)
                v.tensor_tensor(hlo[:, :, o:o + w], src[:, :, o:o + w], hhi[:, :, o:o + w].bitcast(F32),
                                ALU.subtract).then_inc(part_ready, 1)

        def act_tail(act):
            act_part(act, 0, qT, (over[2], 5, 0))
            act.wait_ge(smp_loaded, 96)
            act.activation(smb[:, 1, :, :], smb[:, 1, :, :], ACT.Exp).then_inc(smp_act, 1)
            act.wait_ge(smp_act, 1)
            for i in range(KD):
                b, s = i, i % 2
                act.wait_ge(h0_loaded[s], 16 * (b // 2) + 16)
                if b >= 2:
                    act.wait_ge(hn_stored[s], 16 * (b // 2))
                for k in range(NXB):
                    ins = act.activation(hn[:, s, k, :], h0[:, s, k, :], ACT.Identity, scale=smb[:, 1, k, b:b + 1])
                ins.then_inc(h0_decayed, 1)
                for c, (o, w) in enumerate(CH):
                    act.wait_ge(gemm_done[s], 3 * (ORD_AO + i // 2) + c + 1)
                    act.activation(mixed[:, i, o:o + w], SETS[s][:, c, 0:w], ACT.Identity).then_inc(gemm_evac[s], 1)
            act.wait_ge(ys_ss, 2)
            act.activation(rss[:, :, :], rss[:, :, :], ACT.Sqrt, bias=eps[:, 0:1], scale=1.0 / GW).then_inc(smp_act, 1)
            act_part(act, 1, sraw, (sraw_loaded, 16, 0))
            for i in range(KD):
                for c, (o, w) in enumerate(CH):
                    act.wait_ge(gemm_done[i % 2], 3 * (ORD_SO + i // 2) + c + 1)
                    act.activation(acc[:, i, o:o + w], SETS[i % 2][:, c, 0:w], ACT.Identity)\
                        .then_inc(gemm_evac[i % 2], 1)
            act_part(act, 2, sraw, (sraw_loaded, 32, 0))
            act_part(act, 3, mixed, (mix_ready, 3 * (KD - 1) + 1, 1))
            for j in range(2):
                act.wait_ge(gemm_evac[j], 3 * ORD_FFN2)
            act_norm(act, 2)
            act_ffn(act, 1)
            y_copy(act, 1)

        def y_copy(eng, half):
            for t in range(NT):
                _, _, w = trow(t)
                s = t % 2
                eng.wait_ge(y_T, t + 1)
                if t >= 2:
                    eng.wait_ge(y_stored[s], 16 * (t // 2))
                dst, src = yout[0:w, s, half * 512:(half + 1) * 512], SETS[s][0:w, half, :]
                ins = eng.tensor_copy(dst, src) if half == 0 else eng.activation(dst, src, ACT.Identity)
                ins.then_inc(y_evac[half], 1)

        def dve_tail(v, ch):
            dve_part(v, 0, qT)
            for half in range(2):
                v.wait_ge(bct_done, half + 1)
                v.tensor_copy(bct[:, half * 512:(half + 1) * 512], CD[half][0:NS, :]).then_inc(bct_evac, 1)
            v.wait_ge(smp_loaded, 96)
            v.tensor_tensor(smb[:, 0, :, :], smb[:, 0, :, :], xss[:, 0:NXB, :], ALU.mult).then_inc(smp_dve, 1)
            for b in range(NS):
                s = b % 2
                v.wait_ge(bc_loaded[s], 16 * (b // 2) + 16)
                v.wait_ge(h0_decayed, b + 1)
                v.wait_ge(bx_ready, b + 1)
                v.tensor_tensor(hn[:, s, :, :], hn[:, s, :, :], bx[:, s, :, :], ALU.add).then_inc(hn_ready, 1)
                v.wait_ge(hn_ready, b + 1)
                v.tensor_tensor(h0[:, s, :, :].rearrange("p (g k) n -> p g k n", g=SG),
                                hn[:, s, :, :].rearrange("p (g k) n -> p g k n", g=SG),
                                bcb[:, s, SG * DSTATE:2 * SG * DSTATE].rearrange("p (g n) -> p g n", g=SG).unsqueeze(2)
                                .to_broadcast([P, SG, GB, DSTATE]), ALU.mult).then_inc(ys_done, 1)
                v.wait_ge(ys_done, 2 * b + 1)
                v.tensor_reduce(ys[:, :, b], h0[:, s, :, :], AX_X, ALU.add).then_inc(ys_done, 1)
            v.wait_ge(ys_done, 2 * NS)
            dskb = dsk[:, :].unsqueeze(2).to_broadcast([P, NXB, NS])
            ch.run(v.tensor_tensor(xss[:, 0:NXB, :], xss[:, 0:NXB, :], dskb, ALU.mult))
            ch.run(v.tensor_tensor(ys[:, :, :], ys[:, :, :], xss[:, 0:NXB, :], ALU.add))
            ch.run(v.tensor_tensor(ys[:, :, :], ys[:, :, :], zss[:, :, :], ALU.mult))
            v.tensor_tensor(ysr[:, :, :], ys[:, :, :], ys[:, :, :], ALU.mult).then_inc(smp_dve, 1)
            v.wait_ge(ys_ss, 1)
            v.tensor_reduce(rss[:, :, :], bankC[:, 0:NXB * NS].rearrange("p (g k b) -> p g b k", g=SG, b=NS), AX_X,
                            ALU.add).then_inc(ys_ss, 1)
            v.wait_ge(smp_act, 2)
            ch.run(v.reciprocal(rss[:, :, :], rss[:, :, :]))
            ch.run(v.tensor_tensor(ys[:, :, :].rearrange("p (g k) b -> p g k b", g=SG),
                                   ys[:, :, :].rearrange("p (g k) b -> p g k b", g=SG),
                                   rss[:, :, :].unsqueeze(2).to_broadcast([P, SG, GB, NS]), ALU.mult))
            v.tensor_tensor(ys[:, :, :], ys[:, :, :], gssd[:, :].unsqueeze(2).to_broadcast([P, NXB, NS]), ALU.mult)\
                .then_inc(smp_dve, 1)
            dve_part(v, 1, sraw)
            dve_part(v, 2, sraw)
            for m in range(KD):
                s = m % 2
                for c, (o, w) in enumerate(CH):
                    cs = slice(o, o + w)
                    v.wait_ge(gates_loaded[c], 32 * m + 32)
                    v.tensor_tensor(mixed[:, m, cs], mixed[:, m, cs], gates[:, c, 0, 0:w], ALU.mult)
                    v.wait_ge(gemm_done[s], 3 * (PART_ORD[2] + m // 2) + c + 1)
                    v.tensor_tensor(acc[:, m, cs], acc[:, m, cs], SETS[s][:, c, 0:w], ALU.add).then_inc(gemm_evac[s], 1)
                    v.wait_ge(gemm_evac[s], 3 * (PART_ORD[2] + m // 2) + c + 1)
                    ch.run(v.tensor_tensor(acc[:, m, cs], acc[:, m, cs], gates[:, c, 1, 0:w], ALU.mult))
                    v.tensor_tensor(mixed[:, m, cs], mixed[:, m, cs], acc[:, m, cs], ALU.add).then_inc(mix_ready, 1)
            dve_part(v, 3, mixed)
            v.wait_ge(sraw_loaded, 48)
            for m in range(KD):
                for c, (o, w) in enumerate(CH):
                    v.wait_ge(gemm_done[m % 2], 3 * (ORD_WO + m // 2) + c + 1)
                    v.tensor_tensor(X[:, m, o:o + w], xre[:, m, o:o + w], SETS[m % 2][:, c, 0:w], ALU.add)\
                        .then_inc(gemm_evac[m % 2], 1)
            for j in range(2):
                v.wait_ge(gemm_evac[j], 3 * ORD_FFN2)
            dve_norm(v, 2, ch)
            dve_ffn(v, 1)
            y_copy(v, 0)

        block = ctx.enter_context(nc.Block())

        @block.sync
        def _(sp):
            sp.dma_start(xin[0:META, 0, :], A["meta_tokens"]).then_inc(x_loaded[0], 16)
            sp.dma_start(xin[META:P, 0, :], A["x_prompt"][0, 0:P - META, :]).then_inc(x_loaded[0], 16)
            for t in range(1, NT - 1):
                sp.dma_start(xin[:, t, :], A["x_prompt"][0, t * P - META:(t + 1) * P - META, :]).then_inc(x_loaded[t // 3], 16)
            sp.dma_start(xin[0:LAST, NT - 1, :], A["x_prompt"][0, SEQ - LAST:SEQ, :]).then_inc(x_loaded[2], 16)
            sp.dma_start(xin[LAST:LAST + NS, NT - 1, :], A["x_sample"].rearrange("b s d -> (b s) d"))\
                .then_inc(x_loaded[2], 16)
            sp_ffn(sp, 0)
            sp_in(sp)
            sp_convtail(sp)
            sp_attn(sp)
            sp_ssd(sp)
            sp_tail(sp)

        @block.gpsimd
        def _(pool):
            ch = Chain(pool, pool_seq)
            pool_consts(pool, ch)
            pool_ffn(pool, 0)
            pool_in(pool, ch)
            pool_attn(pool, ch)
            pool_ssd(pool, ch)
            pool_tail(pool, ch)

        @block.tensor
        def _(pe):
            pe.wait_ge(const_ready, 1)
            for t in range(NT):
                o, _, w = trow(t)
                pe.wait_ge(x_loaded[t // 3], 48 if 3 <= t < 6 else 64)
                for half in range(2):
                    u = 2 * t + half
                    if u >= 2:
                        pe.wait_ge(xT_evac, u - 1)
                    for k in range(4):
                        mm = pe.transpose(CD[half][:, k * P:k * P + w], xin[0:w, t, (4 * half + k) * P:(4 * half + k + 1) * P],
                                          ident[0:w, 0:w])
                    mm.then_inc(xT_done, 1)
            pe_norm(pe, 0)
            pe_ffn(pe, 0)
            pe_in(pe)
            pe_convtail(pe)
            pe_attn(pe)
            pe_ssd(pe)
            pe_tail(pe)

        @block.scalar
        def _(act):
            act_params(act)
            act.wait_ge(const_ready, 1)
            act.wait_ge(xT_evac, 2 * NT)
            act_norm(act, 0)
            act_ffn(act, 0)
            act_in(act)
            act_convtail(act)
            act_attn(act)
            act_ssd(act)
            act_tail(act)

        @block.vector
        def _(v):
            ch = Chain(v, dve_seq)
            for t in range(NT):
                o, _, w = trow(t)
                for half in range(2):
                    v.wait_ge(xT_done, 2 * t + half + 1)
                    v.tensor_copy(X[:, 4 * half:4 * half + 4, o:o + w],
                                  CD[half][:, :].rearrange("p (k n) -> p k n", k=4)[:, :, 0:w]).then_inc(xT_evac, 1)
            v.wait_ge(params_loaded, 16 * N_PARAMS)
            dve_norm(v, 0, ch)
            dve_ffn(v, 0)
            dve_in(v, ch)
            dve_convtail(v)
            dve_attn(v, ch)
            dve_ssd(v, ch)
            dve_tail(v, ch)
            v.wait_ge(conv_out[0], 16 * 12)
            v.wait_ge(conv_out[1], 16 * 12)
            v.wait_ge(outs_done, 16 * N_OUT[0])


_INS = ["x_prompt", "x_sample", "cache_k", "cache_v", "cache_kidx", "state_ssm", "state_conv", "page_table",
        "meta_tokens", "g_ffn1", "w_ffn1_gate", "w_ffn1_up", "w_ffn1_down", "g_mix", "w_in", "g_q", "g_k",
        "conv_w", "conv_b", "dt_bias", "a_log", "d_skip", "g_ssd_norm", "w_attn_out", "w_ssd_out", "w_o",
        "g_ffn2", "w_ffn2_gate", "w_ffn2_up", "w_ffn2_down"]
_OUTS = [("y_prompt", (1, SEQ, D)), ("y_sample", (NS, 1, D)),
         ("k_prompt", (1, 1, L, NKV, HD)), ("v_prompt", (1, 1, L, NKV, HD)), ("kidx_prompt", (1, 1, L, HD)),
         ("ssm_prompt", (1, 1, SH, HD, DSTATE)), ("conv_prompt", (1, 1, 3, CONVD)),
         ("k_sample", (1, NS, 1, NKV, HD)), ("v_sample", (1, NS, 1, NKV, HD)), ("kidx_sample", (1, NS, 1, HD)),
         ("ssm_sample", (1, NS, SH, HD, DSTATE)), ("conv_sample", (1, NS, 3, CONVD))]


def kernel(**inputs):
    import numpy as np
    import concourse.bacc as bacc
    from concourse.bass_utils import run_bass_kernel_spmd

    nc = bacc.Bacc("TRN2", target_bir_lowering=False, num_devices=1)
    arrays, ins, outs = {}, {}, {}
    for name in _INS:
        a = np.ascontiguousarray(inputs[name])
        arrays["in_" + name] = a
        ins[name] = nc.dram_tensor("in_" + name, a.shape, mybir.dt.from_np(a.dtype), kind="ExternalInput").ap()
    for name, shape in _OUTS:
        outs[name] = nc.dram_tensor("out_" + name, shape, F32, kind="ExternalOutput").ap()
    build(nc, ins, outs)
    r = run_bass_kernel_spmd(nc, [arrays], core_ids=[0])
    return tuple(r.results[0]["out_" + name] for name, _ in _OUTS)
```
